# Optimizing a Trainium2 kernel written in Bass

```python
import jax, jax.numpy as jnp
from jax import lax
import numpy as np

D_MODEL = 1024
BATCH = 1
SEQ = 512
DEPTH = 2

CHUNK = 64
Q_BLOCK = 128
D_PLE = 256
EPS = 1e-6
SB_HEADS = 8
SB_HEAD_DIM = 64
SB_WIDTH = SB_HEADS * SB_HEAD_DIM
MLA_HEADS = 8
MLA_NOPE = 64
MLA_ROPE = 32
MLA_QK = MLA_NOPE + MLA_ROPE
MLA_V = 64
MLA_Q_RANK = 384
MLA_KV_RANK = 256
MLA_WIDTH = MLA_HEADS * MLA_V
MIX_WIDTH = SB_WIDTH + MLA_WIDTH
ROPE_THETA = 10000.0
SPLITS = [SB_WIDTH, 2 * SB_WIDTH, 3 * SB_WIDTH,
          3 * SB_WIDTH + MLA_Q_RANK,
          3 * SB_WIDTH + MLA_Q_RANK + MLA_KV_RANK]
IN_COLS = 3 * SB_WIDTH + MLA_Q_RANK + MLA_KV_RANK + MLA_ROPE
N_GROUPS = 4
EXPERTS_PER_GROUP = 8
N_EXPERTS = N_GROUPS * EXPERTS_PER_GROUP
TOP_K = 2
D_EXPERT = 256

kernel_name = "hybrid_sb_mla_hmoe_ple_trunk"

def rmsnorm(x, g):
    xf = x.astype(jnp.float32)
    y = xf * lax.rsqrt(jnp.mean(xf * xf, axis=-1, keepdims=True) + EPS)
    return (y * g.astype(jnp.float32)).astype(x.dtype)

def apply_rope(x, cos, sin):
    half = x.shape[-1] // 2
    x1, x2 = x[..., :half], x[..., half:]
    return jnp.concatenate([x1 * cos - x2 * sin, x2 * cos + x1 * sin], axis=-1)

def split_heads(t, n):
    b, s, _ = t.shape
    return t.reshape(b, s, n, -1).transpose(0, 2, 1, 3)

def merge_heads(t):
    b, h, s, d = t.shape
    return t.transpose(0, 2, 1, 3).reshape(b, s, h * d)

def to_blocks(t):
    b, h, s, d = t.shape
    return t.reshape(b, h, s // Q_BLOCK, Q_BLOCK, d).transpose(2, 0, 1, 3, 4)

def from_blocks(t):
    nb, b, h, qb, d = t.shape
    return t.transpose(1, 2, 0, 3, 4).reshape(b, h, nb * qb, d)

def stick_breaking_attention(q, k, v):
    s_len, dh = q.shape[2], q.shape[3]
    scale = dh ** -0.5
    key_idx = jnp.arange(s_len)

    def block(args):
        q_blk, start = args
        z = jnp.einsum("bhqd,bhkd->bhqk", q_blk, k).astype(jnp.float32) * scale
        q_idx = start + jnp.arange(Q_BLOCK)
        mask = key_idx[None, :] < q_idx[:, None]
        log_not = jnp.where(mask, jax.nn.log_sigmoid(-z), 0.0)
        later = lax.cumsum(log_not, axis=3, reverse=True) - log_not
        w = jnp.where(mask, jnp.exp(jax.nn.log_sigmoid(z) + later), 0.0)
        return jnp.einsum("bhqk,bhkd->bhqd", w.astype(v.dtype), v)

    starts = jnp.arange(s_len // Q_BLOCK) * Q_BLOCK
    return from_blocks(lax.map(block, (to_blocks(q), starts)))

def chunk_causal_softmax_attention(q, k, v):
    s_len, dh = q.shape[2], q.shape[3]
    scale = dh ** -0.5
    key_chunk = jnp.arange(s_len) // CHUNK

    def block(args):
        q_blk, start = args
        sc = jnp.einsum("bhqd,bhkd->bhqk", q_blk, k).astype(jnp.float32) * scale
        q_chunk = (start + jnp.arange(Q_BLOCK)) // CHUNK
        mask = key_chunk[None, :] <= q_chunk[:, None]
        pr = jax.nn.softmax(jnp.where(mask, sc, -jnp.inf), axis=-1)
        return jnp.einsum("bhqk,bhkd->bhqd", pr.astype(v.dtype), v)

    starts = jnp.arange(s_len // Q_BLOCK) * Q_BLOCK
    return from_blocks(lax.map(block, (to_blocks(q), starts)))

def hier_moe(x, w_rg, b_rg, w_re, b_re, w_gate, w_up, w_down):
    b, s, d = x.shape
    t = x.reshape(-1, d)
    tf = t.astype(jnp.float32)
    group_p = jax.nn.softmax(tf @ w_rg.astype(jnp.float32) + b_rg.astype(jnp.float32), axis=-1)
    gp, g = lax.top_k(group_p, 1)
    e_logits = (tf @ w_re.astype(jnp.float32) + b_re.astype(jnp.float32)).reshape(-1, N_GROUPS, EXPERTS_PER_GROUP)
    e_logits = jnp.take_along_axis(e_logits, g[:, :, None], axis=1)[:, 0]
    top_l, top_i = lax.top_k(e_logits, TOP_K)
    top_w = jax.nn.softmax(top_l, axis=-1) * gp
    expert_id = g * EXPERTS_PER_GROUP + top_i
    combine = jnp.sum(jax.nn.one_hot(expert_id, N_EXPERTS, dtype=jnp.float32) * top_w[..., None], axis=1)
    y = jnp.zeros_like(tf)
    for e in range(N_EXPERTS):
        hid = jax.nn.silu(t @ w_gate[e]) * (t @ w_up[e])
        y = y + combine[:, e:e + 1] * (hid @ w_down[e]).astype(jnp.float32)
    return y.astype(x.dtype).reshape(b, s, d)

def setup_inputs(seed: int = 0) -> dict:
    key = jax.random.key(seed)
    ks = iter(jax.random.split(key, 32))
    f32 = jnp.float32

    def w(shape, fan_in):
        return jax.random.normal(next(ks), shape, f32) * (fan_in ** -0.5)

    def gain(shape):
        return 1.0 + 0.02 * jax.random.normal(next(ks), shape, f32)

    x = jax.random.normal(next(ks), (BATCH, SEQ, D_MODEL), f32)
    p = jax.random.normal(next(ks), (DEPTH, BATCH, SEQ, D_PLE), f32)
    offsets = jax.random.randint(next(ks), (BATCH,), 0, 1000, dtype=jnp.int32) * CHUNK
    positions = (offsets[:, None] + jnp.arange(SEQ, dtype=jnp.int32)[None, :]).astype(jnp.int32)
    return {
        "x": x,
        "p": p,
        "positions": positions,
        "g_mix": gain((DEPTH, D_MODEL)),
        "w_in": w((DEPTH, D_MODEL, IN_COLS), D_MODEL),
        "g_cq": gain((DEPTH, MLA_Q_RANK)),
        "w_uq": w((DEPTH, MLA_Q_RANK, MLA_HEADS * MLA_QK), MLA_Q_RANK),
        "g_ckv": gain((DEPTH, MLA_KV_RANK)),
        "w_ukv": w((DEPTH, MLA_KV_RANK, MLA_HEADS * (MLA_NOPE + MLA_V)), MLA_KV_RANK),
        "g_osb": gain((DEPTH, SB_WIDTH)),
        "g_omla": gain((DEPTH, MLA_WIDTH)),
        "w_out": w((DEPTH, MIX_WIDTH, D_MODEL), MIX_WIDTH),
        "g_moe": gain((DEPTH, D_MODEL)),
        "w_rg": w((DEPTH, D_MODEL, N_GROUPS), D_MODEL),
        "b_rg": 0.01 * jax.random.normal(next(ks), (DEPTH, N_GROUPS), f32),
        "w_re": w((DEPTH, D_MODEL, N_EXPERTS), D_MODEL),
        "b_re": 0.01 * jax.random.normal(next(ks), (DEPTH, N_EXPERTS), f32),
        "w_gate": w((DEPTH, N_EXPERTS, D_MODEL, D_EXPERT), D_MODEL),
        "w_up": w((DEPTH, N_EXPERTS, D_MODEL, D_EXPERT), D_MODEL),
        "w_down": w((DEPTH, N_EXPERTS, D_EXPERT, D_MODEL), D_EXPERT),
        "g_ple": gain((DEPTH, D_MODEL)),
        "w_pg": w((DEPTH, D_MODEL, D_MODEL), D_MODEL),
        "w_pe": w((DEPTH, D_PLE, D_MODEL), D_PLE),
        "g_final": gain((D_MODEL,)),
    }

def reference(x, p, positions, g_mix, w_in, g_cq, w_uq, g_ckv, w_ukv, g_osb, g_omla,
              w_out, g_moe, w_rg, b_rg, w_re, b_re, w_gate, w_up, w_down,
              g_ple, w_pg, w_pe, g_final):
    b, s, _ = x.shape
    inv_freq = ROPE_THETA ** (-jnp.arange(0, MLA_ROPE, 2, dtype=jnp.float32) / MLA_ROPE)
    ang = positions.astype(jnp.float32)[..., None] * inv_freq
    cos = jnp.cos(ang).astype(x.dtype)
    sin = jnp.sin(ang).astype(x.dtype)

    h = x
    for i in range(DEPTH):
        hn = rmsnorm(h, g_mix[i])
        proj = hn @ w_in[i]
        q_sb, k_sb, v_sb, c_q, c_kv, k_r = jnp.split(proj, SPLITS, axis=-1)

        o_sb = merge_heads(stick_breaking_attention(
            split_heads(q_sb, SB_HEADS), split_heads(k_sb, SB_HEADS), split_heads(v_sb, SB_HEADS)))

        q = (rmsnorm(c_q, g_cq[i]) @ w_uq[i]).reshape(b, s, MLA_HEADS, MLA_QK)
        q_nope, q_rope = q[..., :MLA_NOPE], q[..., MLA_NOPE:]
        q_rope = apply_rope(q_rope, cos[:, :, None, :], sin[:, :, None, :])
        kv = (rmsnorm(c_kv, g_ckv[i]) @ w_ukv[i]).reshape(b, s, MLA_HEADS, MLA_NOPE + MLA_V)
        k_nope, v_mla = kv[..., :MLA_NOPE], kv[..., MLA_NOPE:]
        k_rope = jnp.broadcast_to(apply_rope(k_r, cos, sin)[:, :, None, :], (b, s, MLA_HEADS, MLA_ROPE))
        q_full = jnp.concatenate([q_nope, q_rope], axis=-1).transpose(0, 2, 1, 3)
        k_full = jnp.concatenate([k_nope, k_rope], axis=-1).transpose(0, 2, 1, 3)
        o_mla = merge_heads(chunk_causal_softmax_attention(q_full, k_full, v_mla.transpose(0, 2, 1, 3)))

        mixed = jnp.concatenate([rmsnorm(o_sb, g_osb[i]), rmsnorm(o_mla, g_omla[i])], axis=-1)
        h = h + mixed @ w_out[i]

        h = h + hier_moe(rmsnorm(h, g_moe[i]), w_rg[i], b_rg[i], w_re[i], b_re[i],
                         w_gate[i], w_up[i], w_down[i])

        gate = jax.nn.sigmoid((rmsnorm(h, g_ple[i]) @ w_pg[i]).astype(jnp.float32))
        h = h + (gate * (p[i] @ w_pe[i]).astype(jnp.float32)).astype(h.dtype)

    return rmsnorm(h, g_final)


_drawn_inputs = setup_inputs


def setup_inputs(seed=0):
    import zlib

    import numpy as np

    out = dict(_drawn_inputs(seed))
    spreads = {}
    factors = {'b_rg': 3.927, 'b_re': 2.861, 'g_ple': 28.915, 'g_final': 8.338, 'g_cq': 2.693}
    for name, (base, spread) in spreads.items():
        noise = np.random.default_rng([zlib.crc32(name.encode()), seed]).standard_normal(out[name].shape)
        drawn = base * np.exp(spread * noise) if base else spread * noise
        out[name] = __import__('jax').numpy.asarray(drawn.astype(out[name].dtype))
    for name, factor in factors.items():
        out[name] = (out[name] * factor).astype(out[name].dtype)
    return out
```

```python
def _program(nc, io, out):
    import numpy as np
    import concourse.bass as bass
    from concourse import mybir

    fp32, bf16, i32, u32 = mybir.dt.float32, mybir.dt.bfloat16, mybir.dt.int32, mybir.dt.uint32
    ALU, ACT, AX = mybir.AluOpType, mybir.ActivationFunctionType, mybir.AxisListType

    P = 128
    DEPTH, D = io["g_mix"].shape
    S = io["x"].shape[1]
    NT = S // P
    DC = D // P
    HALF = D // 2
    NH, HD = 8, 64
    NPAIR = NH // 2
    QR, KVR, ROPE = io["g_cq"].shape[1], io["g_ckv"].shape[1], 32
    QC, KVC = QR // P, KVR // P
    QK = HD + ROPE
    SBW = NH * HD
    IN = io["w_in"].shape[2]
    LAT = IN - 3 * SBW
    NG, NE = io["w_rg"].shape[2], io["w_re"].shape[2]
    NR = NG + NE
    EG = NE // NG
    DE = io["w_gate"].shape[3]
    EC = DE // P
    SLOT = 64
    PAIRS = NE // 2
    MAIN = NE * SLOT
    XTRA = 2 * S // (SLOT + 1)
    PE_IN = io["p"].shape[3]
    PC = PE_IN // P
    CHUNK = 64
    EPS = 1e-6
    BIG = 1e30
    ROUND = 1.5 * 2.0 ** 23
    SB_SCALE, MLA_SCALE = HD ** -0.5, QK ** -0.5

    xn_rows = nc.dram_tensor("xn_rows", [S, D], fp32, kind="Internal").ap()
    y_rows = nc.dram_tensor("y_rows", [MAIN + XTRA * SLOT, D], fp32, kind="Internal").ap()

    W_IN = DC * IN
    words = nc.alloc_sbuf_tensor("words", [P, 50560], fp32)

    def cut(at, *shape):
        n = int(np.prod(shape))
        v = words[:, at:at + n]
        if len(shape) == 2:
            v = v.rearrange("p (a b) -> p a b", a=shape[0])
        if len(shape) == 3:
            v = v.rearrange("p (a b c) -> p a b c", a=shape[0], b=shape[1])
        return v

    h = cut(0, NT, D)
    ARENA = NT * D
    w_qk = cut(ARENA, DC, 2 * SBW)
    w_vl = cut(ARENA + DC * 2 * SBW, DC, IN - 2 * SBW)
    EXPERT = 2 * DC * DE + EC * D
    w_gu = [cut(ARENA + s * EXPERT, 2, DC, DE) for s in range(4)]
    w_dn = [cut(ARENA + s * EXPERT + 2 * DC * DE, EC, D) for s in range(4)]
    w_o = cut(ARENA + 2 * EXPERT, 2 * NPAIR, D)
    w_uq = cut(ARENA + 2 * EXPERT + DC * D, QC, NH * QK)
    w_ukv = cut(ARENA + 2 * EXPERT + DC * D + QC * NH * QK, KVC, NH * 2 * HD)
    w_e = cut(ARENA + 3 * EXPERT, PC, D)
    p_tok = cut(ARENA + 3 * EXPERT + PC * D, NT, PE_IN)
    pT = cut(ARENA + 3 * EXPERT + PC * D + NT * PE_IN, PC, S)
    XT = ARENA + 2 * EXPERT + DC * D + QC * NH * QK + KVC * NH * 2 * HD
    xT = cut(XT, DC, S)
    kT = cut(XT, NH, S)
    XN = XT + DC * S
    xn = [cut(XN + b * D, D) for b in range(2)]
    q_tok = cut(XN, NH, QK)
    k_tok = cut(XN + D, NH, QK)
    LATENT = XN + 2 * D
    lat = cut(LATENT, NT, LAT)
    ATT = LATENT + NT * LAT
    qT_sb = cut(ATT, NPAIR, S)
    kT_sb = cut(ATT + NPAIR * S, NPAIR, S)
    qT = cut(ATT, NH, S)
    v_att = cut(ATT + 2 * NPAIR * S, NT, SBW)
    oT = cut(ATT + 2 * NPAIR * S + NT * SBW, 2 * NPAIR, S)
    cqT = cut(ATT + 2 * NPAIR * S + NT * SBW + 2 * NPAIR * S, QC, S)
    ckvT = cut(ATT + 2 * NPAIR * S + NT * SBW + 2 * NPAIR * S + QC * S, KVC, S)
    rope_t = cut(ATT + 2 * NPAIR * S + NT * SBW + (2 * NPAIR - 1) * S, 4, NH, ROPE // 2)
    stay = cut(XT, 2, 2, S + 2)
    take = cut(XT + 4 * (S + 2), 2, 2, S)
    wT = cut(XT + 4 * (S + 2) + 4 * S, 2, 2, S)
    prob = cut(XN, 2, 2, S)
    pTr = cut(XN + 4 * S, 2, 2, S)
    o_square = [cut(XT + 4 * (S + 2) + 8 * S, 2, S), cqT[:, 0:2, :]]
    o_total = [cut(XT + 4 * (S + 2) + 10 * S, S), cqT[:, 2, :]]
    xg = [cut(LATENT + b * D, D) for b in range(2)]
    xgT = [cut(LATENT + (2 + b) * D, DC, P) for b in range(2)]
    y_out = [cut(LATENT + (4 + b) * D, D) for b in range(2)]
    back = [cut(LATENT + b * D, D) for b in range(4)]
    w_g = cut(LATENT + 6 * D, DC, D)
    silu = [cut(XN + b * 3 * DE, DE) for b in range(2)]
    hid = [cut(XN + b * 3 * DE + DE, DE) for b in range(2)]
    hidT = [cut(XN + b * 3 * DE + 2 * DE, EC, P) for b in range(2)]
    R0 = LATENT + 4 * D
    sel_rank = cut(R0, 2 * NT, P)
    sel_tok = cut(R0 + 2 * NT * P, 2 * NT, NE)
    R1 = R0 + 2 * NT * P + 2 * NT * NE
    logit = cut(R1, NT, NR)
    g8 = cut(R1 + 144, NT, 8)
    rank = cut(R1 + 176, NT, NE)
    rtmp = cut(R1 + 304, NT, NE)
    over = cut(R1 + 432, NT, NE)
    best8 = cut(R1 + 560, NT, 8)
    extra = cut(R1 + 592, NE)
    extra_sum = cut(R1 + 624, NE)
    shift = cut(R1 + 656, NE)
    gsc = cut(R1 + 688, NT, 8)
    steps7 = cut(R0, NE, 7)
    steps15 = cut(R0 + 256, 16, NE)
    gate_s = [cut(LATENT + 4 * D + b * HALF, HALF) for b in range(2)]
    sel_x = cut(LATENT + 5 * D, 2 * NT, SLOT)
    g_last = cut(XT, D)

    def sb(name, shape, dt=fp32):
        return nc.alloc_sbuf_tensor(name, [P] + list(shape), dt)

    ident, ones = sb("ident", [P]), sb("ones", [P])
    ident_b, ones_b, before_b = sb("ident_b", [P], bf16), sb("ones_b", [P], bf16), sb("before_b", [P], bf16)
    sb_mask, mla_mask = sb("sb_mask", [P], bf16), sb("mla_mask", [P], bf16)
    junk = sb("junk", [D], bf16)
    cos, sin = sb("cos", [NT, ROPE // 2]), sb("sin", [NT, ROPE // 2])
    slot_no, expert_no, tok_no = sb("slot_no", [P]), sb("expert_no", [NE]), sb("tok_no", [NT])
    thresh, xtra_no = sb("thresh", [7]), sb("xtra_no", [16])
    minus_half = sb("minus_half", [8])
    g_norm = sb("g_norm", [3, DEPTH, DC])
    g_lat = sb("g_lat", [DEPTH, QC + KVC])
    g_o = sb("g_o", [DEPTH, 2 * NPAIR])
    b_r = sb("b_r", [DEPTH, NR])
    w_r = sb("w_r", [DC, NR])
    pos_i, pos_f = sb("pos_i", [NT], i32), sb("pos_f", [NT])
    inv_freq = sb("inv_freq", [ROPE // 2])
    ang, turn, red = (cut(XT + k * NT * ROPE // 2, NT, ROPE // 2) for k in range(3))
    k_rot = sb("k_rot", [NT, ROPE])
    ms, rstd = sb("ms", [16]), sb("rstd", [16])
    ms_lat, rstd_lat = sb("ms_lat", [NT, 2]), sb("rstd_lat", [NT, 2])
    ms_o, rstd_o = sb("ms_o", [2, NT]), sb("rstd_o", [2, NT])
    peak, rsum, rinv = sb("peak", [2, 2]), sb("rsum", [2, 2]), sb("rinv", [2, 2])
    memb_b = sb("memb_b", [NT, NE], bf16)
    best_i, g_i = sb("best_i", [NT, 8], u32), sb("g_i", [NT, 8], u32)
    best_f, g_f = sb("best_f", [NT, 2]), sb("g_f", [NT])
    chosen = sb("chosen", [2, NT, NE])
    rank_f = sb("rank_f", [2, NT])
    gp, top_w = sb("gp", [NT]), sb("top_w", [2, NT])
    slot_f, slot_i = sb("slot_f", [2, NT]), sb("slot_i", [2, NT], i32)
    slot_x = sb("slot_x", [2, NT])
    tok_i = sb("tok_i", [PAIRS], i32)
    tokx_i = sb("tokx_i", [1], i32)
    xtra_i = sb("xtra_i", [2 + 16], i32)
    xtra_f = sb("xtra_f", [2 + 16])

    bank = nc.alloc_psum_tensor("bank", [P, 8, 512], fp32)

    def ps(b, n=512, off=0, lo=0, hi=P):
        return bank[lo:hi, b, off:off + n]

    def ps2(b, n):
        return bank[:, b:b + 2, :].rearrange("p a b -> p (a b)")[:, 0:n]

    class Signal:

        def __init__(self, name, per_layer, credit=0):
            self.sem, self.per_layer, self.credit = nc.alloc_semaphore(name), per_layer, credit

        def at(self, L, k):
            return L * self.per_layer + (self.credit + k)

    STEPS_DVE, STEPS_POOL, STEPS_ACT = 145, 19, 48
    NORMS = 3 * NT
    const_ready = Signal("const_ready", 0)
    loaded = Signal("loaded", 0)
    gains_in = Signal("gains_in", 0)
    r_in = Signal("r_in", 2 * 16)
    rope_ready = Signal("rope_ready", 0)
    h_moe = Signal("h_moe", NT)
    squared = Signal("squared", NORMS)
    rooted = Signal("rooted", NORMS)
    xn_ready = Signal("xn_ready", NORMS)
    flipped = Signal("flipped", NORMS)
    xT_ready = Signal("xT_ready", 2 * NORMS)
    qk_done = Signal("qk_done", 2 * NPAIR)
    qk_act, qk_dve = Signal("qk_act", NPAIR), Signal("qk_dve", NPAIR)
    vl_done = Signal("vl_done", NT)
    v_out, lat_out = Signal("v_out", NT), Signal("lat_out", NT)
    lat_sq, lat_root, lat_ready = Signal("lat_sq", NT), Signal("lat_root", NT), Signal("lat_ready", NT)
    lat_flip = Signal("lat_flip", 1)
    cqT_ready, ckvT_ready = Signal("cqT_ready", 1), Signal("ckvT_ready", 1)
    UNITS = NPAIR * NT
    sb_z, sb_sig, sb_w = Signal("sb_z", UNITS), Signal("sb_sig", 2 * UNITS), Signal("sb_w", 2 * UNITS)
    sb_scan = Signal("sb_scan", 2 * UNITS)
    sb_flip = Signal("sb_flip", UNITS)
    sb_wT = [Signal("sb_wT0", UNITS), Signal("sb_wT1", UNITS)]
    sb_o = Signal("sb_o", UNITS)
    up_done, q_out, k_out = Signal("up_done", 2 * NT), Signal("q_out", NT), Signal("k_out", NT)
    q_rope, k_rope = Signal("q_rope", NT), Signal("k_rope", NT)
    up_flip, qT_out, kT_out = Signal("up_flip", 2 * NT), Signal("qT_out", 2 * NT), Signal("kT_out", 2 * NT)
    ml_z, ml_peak, ml_exp = Signal("ml_z", UNITS), Signal("ml_peak", 2 * UNITS), Signal("ml_exp", 2 * UNITS)
    ml_w, ml_flip = Signal("ml_w", 2 * UNITS), Signal("ml_flip", UNITS)
    ml_wT = [Signal("ml_wT0", UNITS), Signal("ml_wT1", UNITS)]
    ml_o = Signal("ml_o", UNITS)
    o_sq, o_sum = Signal("o_sq", 2 * NPAIR), Signal("o_sum", 2 * NPAIR)
    o_ms, o_ms_out, o_root = Signal("o_ms", 2), Signal("o_ms_out", 2), Signal("o_root", 2)
    wo_done, wo_out = Signal("wo_done", 2 * NT), Signal("wo_out", 2 * NT)
    xn_stored = [Signal(f"xn_stored{b}", 16 * NT // 2) for b in range(2)]
    r_done, r_out = Signal("r_done", NT), Signal("r_out", 1)
    g_exp, e_in, e_exp = Signal("g_exp", 1), Signal("e_in", 2), Signal("e_exp", 1)
    memb_ready, rank_done = Signal("memb_ready", 1), Signal("rank_done", 1)
    sel_ready, tok_done, tok_ready = Signal("sel_ready", 1), Signal("tok_done", 1), Signal("tok_ready", 1)
    slots_ready = Signal("slots_ready", 1)
    w_in_in = Signal("w_in_in", 2 * 16)
    w_up_in, w_o_in = Signal("w_up_in", 2 * 16), Signal("w_o_in", 16)
    gu_in = [Signal(f"gu_in{b}", 2 * 16 * PAIRS // 2) for b in range(2)]
    dn_in = [Signal(f"dn_in{b}", 16 * PAIRS // 2) for b in range(2)]
    gathered = [Signal(f"gathered{b}", 16 * PAIRS // 2) for b in range(2)]
    g_flip, xgT_ready = Signal("g_flip", PAIRS), Signal("xgT_ready", 2 * PAIRS)
    gu_done, silu_done, hid_ready = Signal("gu_done", PAIRS), Signal("silu_done", PAIRS), Signal("hid_ready", PAIRS)
    hid_flip, hidT_ready = Signal("hid_flip", PAIRS), Signal("hidT_ready", PAIRS)
    dn_done = Signal("dn_done", PAIRS)
    y_act, y_dve = Signal("y_act", PAIRS, 1), Signal("y_dve", PAIRS, 1)
    y_stored = [Signal(f"y_stored{b}", 16 * PAIRS // 2, 1) for b in range(2)]
    x_sel, x_tok, x_idx, x_gather, x_w = [nc.alloc_semaphore(n) for n in ("x_sel", "x_tok", "x_idx", "x_gather", "x_w")]
    x_flip, x_T, x_gu, x_silu, x_hid = [nc.alloc_semaphore(n) for n in ("x_flip", "x_T", "x_gu", "x_silu", "x_hid")]
    x_hflip, x_hT, x_dn, x_y, x_store = [nc.alloc_semaphore(n) for n in ("x_hflip", "x_hT", "x_dn", "x_y", "x_store")]
    x_over = Signal("x_over", 1)
    back_in = [Signal(f"back_in{b}", 16 * NT) for b in range(2)]
    w_g_in, w_e_in = Signal("w_g_in", 16), Signal("w_e_in", 2 * 16)
    p_flip, pT_ready = Signal("p_flip", PC), Signal("pT_ready", PC)
    gate_done, gate_out = Signal("gate_done", 2 * NT), Signal("gate_out", 2 * NT)
    pe_done, ple_out = Signal("pe_done", 2 * NT, 1), Signal("ple_out", 2 * NT, 2 * NT)
    act_step, dve_step, pool_step = Signal("act_step", STEPS_ACT), Signal("dve_step", STEPS_DVE), Signal("pool_step", STEPS_POOL)
    fin_eps = nc.alloc_semaphore("fin_eps")
    fin_sq, fin_root, fin_ready = Signal("fin_sq", 0), Signal("fin_root", 0), Signal("fin_ready", 0)
    g_last_in, stored = Signal("g_last_in", 0), Signal("stored", 0)

    filled = nc.alloc_semaphore("filled")
    passed = nc.alloc_semaphore("passed")

    def alone(eng):
        eng.sem_inc(passed, 1)

    class Steps:

        def __init__(self, eng, counted):
            self.eng, self.counted, self.n = eng, counted, 0

        def add(self, L):
            self.n += 1
            return self.counted.sem

        def wait(self, L, back=0):
            self.eng.wait_ge(self.counted.sem, self.counted.at(L, self.n - back))

    with nc.Block() as block:

        @block.sync
        def _(sp):
            x_v = io["x"][0].rearrange("(t p) d -> p t d", p=P)
            sp.dma_start(h, x_v).then_inc(loaded.sem, 16)
            sp.dma_start(pos_i[:], io["positions"][0].rearrange("(t p) -> p t", p=P),
                         allow_slow_non_contiguous=True).then_inc(loaded.sem, 16)
            w_in_v = io["w_in"].rearrange("l (p c) n -> l p c n", c=DC)
            gate_v = io["w_gate"].rearrange("l (n e) (p c) f -> (l n) p e (c f)", e=2, c=DC)
            up_v = io["w_up"].rearrange("l (n e) (p c) f -> (l n) p e (c f)", e=2, c=DC)
            down_v = io["w_down"].rearrange("l (n e) (p c) f -> (l n) p e (c f)", e=2, c=EC)
            xn_v = xn_rows.rearrange("(t p) d -> t p d", p=P)
            for k, name in enumerate(("g_mix", "g_moe", "g_ple")):
                sp.dma_start(g_norm[:, k], io[name].rearrange("l (p c) -> p l c", c=DC)).then_inc(gains_in.sem, 16)
            for to, name in ((g_lat[:, :, 0:QC], "g_cq"), (g_lat[:, :, QC:QC + KVC], "g_ckv"),
                             (g_o[:, :, 0:NPAIR], "g_osb"), (g_o[:, :, NPAIR:2 * NPAIR], "g_omla")):
                for l in range(DEPTH):
                    sp.dma_start(to[:, l], io[name][l].rearrange("(c p) -> p c", p=P),
                                 allow_slow_non_contiguous=True).then_inc(gains_in.sem, 16)
            for l in range(DEPTH):
                sp.dma_start(b_r[:, l, 0:NG], io["b_rg"][l].unsqueeze(0).to_broadcast([P, NG])).then_inc(gains_in.sem, 16)
                sp.dma_start(b_r[:, l, NG:NR], io["b_re"][l].unsqueeze(0).to_broadcast([P, NE])).then_inc(gains_in.sem, 16)
            with sp.Fori(0, DEPTH) as L:
                sp.dma_start(w_qk, w_in_v[L][:, :, 0:2 * SBW]).then_inc(w_in_in.sem, 16)
                sp.dma_start(w_vl, w_in_v[L][:, :, 2 * SBW:IN]).then_inc(w_in_in.sem, 16)
                sp.dma_start(w_r[:, :, 0:NG], io["w_rg"].rearrange("l (p c) n -> l p c n", c=DC)[L]).then_inc(r_in.sem, 16)
                sp.dma_start(w_r[:, :, NG:NR], io["w_re"].rearrange("l (p c) n -> l p c n", c=DC)[L]).then_inc(r_in.sem, 16)
                with sp.If(L < 1):
                    sp.wait_ge(w_in_in.sem, 2 * 16)
                    fill = XTRA * SLOT * D // P
                    sp.dma_start(y_rows[MAIN:].rearrange("r d -> (r d)").rearrange("(p f) -> p f", p=P),
                                 words[:, ARENA:ARENA + fill]).then_inc(filled, 16)
                sp.nop()
                sp.wait_ge(pe_done.sem, pe_done.at(L, 0))
                sp.dma_start(w_uq, io["w_uq"].rearrange("l (c p) n -> l p c n", p=P)[L]).then_inc(w_up_in.sem, 16)
                sp.dma_start(w_ukv, io["w_ukv"].rearrange("l (c p) n -> l p c n", p=P)[L]).then_inc(w_up_in.sem, 16)
                sp.wait_ge(vl_done.sem, vl_done.at(L, NT))
                sp.wait_ge(filled, 16)
                sp.dma_start(w_o, io["w_out"].rearrange("l (c p) n -> l p c n", p=P)[L]).then_inc(w_o_in.sem, 16)

                def load_pair(n, b):
                    two = words[:, ARENA + 2 * b * EXPERT:ARENA + (2 * b + 2) * EXPERT].rearrange("p (e w) -> p e w", e=2)
                    sp.dma_start(two[:, :, 0:DC * DE], gate_v[L * PAIRS + n]).then_inc(gu_in[b].sem, 16)
                    sp.dma_start(two[:, :, DC * DE:2 * DC * DE], up_v[L * PAIRS + n]).then_inc(gu_in[b].sem, 16)
                    sp.dma_start(two[:, :, 2 * DC * DE:EXPERT], down_v[L * PAIRS + n]).then_inc(dn_in[b].sem, 16)

                load_pair(0, 0)
                sp.wait_ge(wo_done.sem, wo_done.at(L, 2 * NT))
                load_pair(1, 1)
                sp.dma_start(w_g, io["w_pg"].rearrange("l (p c) n -> l p c n", c=DC)[L]).then_inc(w_g_in.sem, 16)
                for t in range(NT):
                    sp.wait_ge(xn_ready.sem, xn_ready.at(L, NT + t + 1))
                    sp.dma_start(xn_v[t], xn[t % 2]).then_inc(xn_stored[t % 2].sem, 16)
                with sp.Fori(0, PAIRS // 2 - 1) as i:
                    for b in range(2):
                        sp.wait_ge(dn_done.sem, dn_done.at(L, 2 * i + b + 1))
                        load_pair(2 * i + (b + 2), b)
                sp.wait_ge(slots_ready.sem, slots_ready.at(L, 1))
                alone(sp)
                so_far = sp.value_load(xtra_i[0:1, 0:1], min_val=0, max_val=DEPTH * XTRA)
                n_xtra = sp.value_load(xtra_i[0:1, 1:2], min_val=0, max_val=XTRA)
                e_v = [io[n].rearrange("l e (p c) f -> (l e) p (c f)", p=P) for n in ("w_gate", "w_up", "w_down")]
                with sp.Fori(0, XTRA) as j:
                    with sp.If(j < n_xtra):
                        sp.wait_ge(x_idx, so_far + j + 1)
                        alone(sp)
                        e = sp.value_load(xtra_i[0:1, bass.ds(j + 2, 1)], min_val=0, max_val=NE - 1)
                        one = words[:, ARENA:ARENA + EXPERT]
                        sp.dma_start(one[:, 0:DC * DE], e_v[0][L * NE + e]).then_inc(x_w, 16)
                        sp.dma_start(one[:, DC * DE:2 * DC * DE], e_v[1][L * NE + e]).then_inc(x_w, 16)
                        sp.dma_start(one[:, 2 * DC * DE:EXPERT], e_v[2][L * NE + e]).then_inc(x_w, 16)
                    sp.nop()
                sp.wait_ge(dn_done.sem, dn_done.at(L, PAIRS))
                sp.wait_ge(x_over.sem, x_over.at(L, 1))
                sp.dma_start(w_e, io["w_pe"].rearrange("l (p c) n -> l p c n", c=PC)[L]).then_inc(w_e_in.sem, 16)
                sp.dma_start(p_tok, io["p"].rearrange("l b (t p) n -> (l b) p t n", p=P)[L]).then_inc(w_e_in.sem, 16)
            sp.wait_ge(pe_done.sem, pe_done.at(DEPTH, 0))
            sp.dma_start(g_last, io["g_final"].unsqueeze(0).to_broadcast([P, D])).then_inc(g_last_in.sem, 16)
            for t in range(NT):
                sp.wait_ge(fin_ready.sem, t + 1)
                sp.dma_start(out[0].rearrange("(t p) d -> t p d", p=P)[t], h[:, t]).then_inc(stored.sem, 16)
            sp.wait_ge(stored.sem, 16 * NT)

        @block.gpsimd
        def _(pool):
            step = Steps(pool, pool_step)
            made = nc.alloc_semaphore("made")
            pool.memset(ident[:], 0.0).then_inc(made, 1)
            pool.memset(sb_mask[:], 0.0).then_inc(made, 1)
            pool.memset(mla_mask[:], 0.0).then_inc(made, 1)
            pool.memset(before_b[:], 1.0).then_inc(made, 1)
            pool.wait_ge(made, 4)
            pool.affine_select(out=ident[:], in_=ident[:], compare_op=ALU.not_equal, fill=1.0, base=0,
                               pattern=[[-1, P]], channel_multiplier=1).then_inc(made, 1)
            pool.affine_select(out=sb_mask[:], in_=sb_mask[:], compare_op=ALU.is_gt, fill=-BIG, base=0,
                               pattern=[[-1, P]], channel_multiplier=1).then_inc(made, 1)
            pool.memset(mla_mask[0:CHUNK, CHUNK:P], -BIG).then_inc(made, 1)
            pool.affine_select(out=before_b[:], in_=before_b[:], compare_op=ALU.is_gt, fill=0.0, base=0,
                               pattern=[[1, P]], channel_multiplier=-1).then_inc(made, 1)
            pool.wait_ge(made, 8)
            pool.tensor_copy(ident_b[:], ident[:]).then_inc(made, 1)
            pool.memset(ones[:], 1.0).then_inc(made, 1)
            pool.memset(ones_b[:], 1.0).then_inc(made, 1)
            pool.memset(minus_half[:], -0.5).then_inc(made, 1)
            pool.memset(xtra_i[:], 0).then_inc(made, 1)
            pool.memset(xtra_f[:], 0.0).then_inc(made, 1)
            pool.iota(slot_no[:], [[0, 2], [1, SLOT]], base=0, channel_multiplier=0,
                      allow_small_or_imprecise_dtypes=True).then_inc(made, 1)
            pool.iota(expert_no[:], [[1, NE]], base=0, channel_multiplier=0,
                      allow_small_or_imprecise_dtypes=True).then_inc(made, 1)
            pool.iota(tok_no[:], [[P, NT]], base=0, channel_multiplier=1,
                      allow_small_or_imprecise_dtypes=True).then_inc(made, 1)
            pool.iota(thresh[:], [[SLOT, 7]], base=SLOT, channel_multiplier=0,
                      allow_small_or_imprecise_dtypes=True).then_inc(made, 1)
            pool.iota(xtra_no[:], [[1, 16]], base=0, channel_multiplier=0,
                      allow_small_or_imprecise_dtypes=True).then_inc(made, 1)
            for k in range(ROPE // 2):
                freq = np.float32(10000.0) ** (-np.float32(2 * k) / np.float32(ROPE))
                pool.memset(inv_freq[:, k:k + 1], float(freq)).then_inc(made, 1)
            pool.wait_ge(made, 19 + ROPE // 2)
            pool.sem_inc(const_ready.sem, 1)

            def root(to, of, before, value, done):
                pool.wait_ge(before.sem, value)
                n = of.shape[1]
                alone(pool)
                pool.tensor_scalar(of, of, EPS, None, ALU.add).then_inc(step.add(0), 1)
                step.wait(layer[0])
                pool.tensor_tensor(to, of, minus_half[:, 0:n], ALU.pow).then_inc(done.sem, 1)

            layer = [None]
            with pool.Fori(0, DEPTH) as L:
                layer[0] = L
                step.n = 0
                for t in range(NT):
                    root(rstd[:, t:t + 1], ms[:, t:t + 1], squared, squared.at(L, t + 1), rooted)
                for t in range(NT):
                    root(rstd_lat[:, t], ms_lat[:, t], lat_sq, lat_sq.at(L, t + 1), lat_root)
                pool.wait_ge(vl_done.sem, vl_done.at(L, NT))
                alone(pool)
                pool.memset(stay[:, :, :, S:S + 2].rearrange("p a b c -> p (a b) c"), 1.0).then_inc(step.add(L), 1)
                step.wait(L)

                def add_squares(kind, m):
                    pool.wait_ge(o_sq.sem, o_sq.at(L, kind * NPAIR + m + 1))
                    if m == 0:
                        alone(pool)
                        pool.tensor_copy(o_total[kind], o_square[kind][:, m % 2]).then_inc(o_sum.sem, 1)
                    else:
                        pool.wait_ge(o_sum.sem, o_sum.at(L, kind * NPAIR + m))
                        pool.tensor_tensor(o_total[kind], o_total[kind], o_square[kind][:, m % 2], ALU.add).then_inc(o_sum.sem, 1)

                for u in range(UNITS):
                    n = (u % NT + 1) * P
                    for s in range(2):
                        pool.wait_ge(sb_scan.sem, sb_scan.at(L, 2 * u + s + 1))
                        pool.tensor_tensor(take[:, u % 2, s, S - n:S], take[:, u % 2, s, S - n:S],
                                           stay[:, u % 2, s, S - n + 1:S + 1], ALU.mult).then_inc(sb_w.sem, 1)
                    if u % NT == 1 and u > NT:
                        add_squares(0, u // NT - 1)
                add_squares(0, NPAIR - 1)
                root(rstd_o[:, 0], ms_o[:, 0], o_ms_out, o_ms_out.at(L, 1), o_root)
                for m in range(NPAIR):
                    add_squares(1, m)
                root(rstd_o[:, 1], ms_o[:, 1], o_ms_out, o_ms_out.at(L, 2), o_root)
                for t in range(NT, 2 * NT):
                    root(rstd[:, t:t + 1], ms[:, t:t + 1], squared, squared.at(L, t + 1), rooted)

                pool.wait_ge(tok_ready.sem, tok_ready.at(L, 1))
                for b in range(2):
                    pool.wait_ge(xn_stored[b].sem, xn_stored[b].at(L, 16 * NT // 2))
                for b in range(2):
                    alone(pool)
                    pool.indirect_dma_start(out=xg[b], out_offset=None, in_=xn_rows,
                                            in_offset=bass.IndirectOffsetOnAxis(ap=tok_i[:, b:b + 1], axis=0)
                                            ).then_inc(gathered[b].sem, 16)
                for n in range(2, PAIRS):
                    pool.wait_ge(g_flip.sem, g_flip.at(L, n - 1))
                    alone(pool)
                    pool.indirect_dma_start(out=xg[n % 2], out_offset=None, in_=xn_rows,
                                            in_offset=bass.IndirectOffsetOnAxis(ap=tok_i[:, n:n + 1], axis=0)
                                            ).then_inc(gathered[n % 2].sem, 16)
                pool.wait_ge(slots_ready.sem, slots_ready.at(L, 1))
                alone(pool)
                so_far = pool.value_load(xtra_i[0:1, 0:1], min_val=0, max_val=DEPTH * XTRA)
                n_xtra = pool.value_load(xtra_i[0:1, 1:2], min_val=0, max_val=XTRA)
                with pool.Fori(0, XTRA) as j:
                    with pool.If(j < n_xtra):
                        pool.wait_ge(x_idx, so_far + j + 1)
                        alone(pool)
                        pool.indirect_dma_start(out=xg[0][0:SLOT], out_offset=None, in_=xn_rows,
                                                in_offset=bass.IndirectOffsetOnAxis(ap=tokx_i[0:SLOT, :], axis=0)
                                                ).then_inc(x_gather, 16)
                    pool.nop()
                pool.wait_ge(x_over.sem, x_over.at(L, 1))
                for t in range(NT):
                    if t >= 2:
                        pool.wait_ge(h_moe.sem, h_moe.at(L, t - 1))
                    for a in range(2):
                        alone(pool)
                        pool.indirect_dma_start(out=back[2 * (t % 2) + a], out_offset=None, in_=y_rows,
                                                in_offset=bass.IndirectOffsetOnAxis(ap=slot_i[:, a, t:t + 1], axis=0)
                                                ).then_inc(back_in[t % 2].sem, 16)
                for t in range(2 * NT, 3 * NT):
                    root(rstd[:, t:t + 1], ms[:, t:t + 1], squared, squared.at(L, t + 1), rooted)
            assert step.n == STEPS_POOL
            for t in range(NT):
                pool.wait_ge(fin_sq.sem, t + 1)
                pool.tensor_scalar(ms[:, 12 + t:13 + t], ms[:, 12 + t:13 + t], EPS, None, ALU.add).then_inc(fin_eps, 1)
                pool.wait_ge(fin_eps, t + 1)
                pool.tensor_tensor(rstd[:, 12 + t:13 + t], ms[:, 12 + t:13 + t], minus_half[:, 0:1], ALU.pow).then_inc(fin_root.sem, 1)

        @block.scalar
        def _(act):
            step = Steps(act, act_step)
            act.sem_inc(y_act.sem, 1)
            for b in range(2):
                act.sem_inc(y_stored[b].sem, 1)
            act.wait_ge(rope_ready.sem, 2)
            act.activation(sin[:].rearrange("p a b -> p (a b)"), red[:].rearrange("p a b -> p (a b)"), ACT.Sin).then_inc(rope_ready.sem, 1)
            act.activation(cos[:].rearrange("p a b -> p (a b)"), turn[:].rearrange("p a b -> p (a b)"), ACT.Sin).then_inc(rope_ready.sem, 1)

            with act.Fori(0, DEPTH) as L:
                step.n = 0

                def mean_squares(stage, source, per):
                    for t in range(NT):
                        n = stage * NT + t
                        act.wait_ge(source.sem, source.at(L, per * (t + 1) - (2 * NT if stage == 0 else 0)))
                        act.activation(junk[:], h[:, t], ACT.Square, scale=D ** -0.5,
                                       accum_out=ms[:, n:n + 1]).then_inc(squared.sem, 1)
                        act.wait_ge(squared.sem, squared.at(L, n + 1))

                mean_squares(0, ple_out, 2)
                for k in range(NPAIR):
                    m = 2 * k
                    act.wait_ge(qk_done.sem, qk_done.at(L, m + 1))
                    to = qT_sb[:, m] if m < NPAIR else kT_sb[:, m - NPAIR]
                    act.activation(to, ps(4 + m % 4), ACT.Copy).then_inc(qk_act.sem, 1)
                for t in range(NT):
                    act.wait_ge(vl_done.sem, vl_done.at(L, t + 1))
                    act.activation(v_att[:, t], ps(2 + 3 * (t % 2)), ACT.Copy).then_inc(v_out.sem, 1)
                    act.wait_ge(lat_out.sem, lat_out.at(L, t + 1))
                    act.activation(junk[:, 0:QR], lat[:, t, 0:QR], ACT.Square, scale=QR ** -0.5,
                                   accum_out=ms_lat[:, t, 0:1]).then_inc(step.add(L), 1)
                    step.wait(L)
                    act.activation(junk[:, 0:KVR], lat[:, t, QR:QR + KVR], ACT.Square, scale=KVR ** -0.5,
                                   accum_out=ms_lat[:, t, 1:2]).then_inc(lat_sq.sem, 1)
                    act.wait_ge(lat_sq.sem, lat_sq.at(L, t + 1))
                act.wait_ge(lat_flip.sem, lat_flip.at(L, 1))
                act.wait_ge(gains_in.sem, 16 * (3 + 6 * DEPTH))
                for j in range(QC):
                    to = act.activation(cqT[:, j], ps(3 + j), ACT.Copy, scale=g_lat[:, L, j:j + 1])
                to.then_inc(cqT_ready.sem, 1)

                def pair_out(kind, m, done):
                    k = kind * NPAIR + m
                    act.wait_ge(done.sem, done.at(L, (m + 1) * NT))
                    act.activation(oT[:, k], ps(6 + m % 2), ACT.Copy, scale=g_o[:, L, k:k + 1]).then_inc(step.add(L), 1)
                    if m >= 2:
                        act.wait_ge(o_sum.sem, o_sum.at(L, k - 1))
                    act.activation(o_square[kind][:, m % 2], ps(6 + m % 2), ACT.Square).then_inc(o_sq.sem, 1)

                for u in range(UNITS + 1):
                    if u < UNITS:
                        n = (u % NT + 1) * P
                        act.wait_ge(sb_z.sem, sb_z.at(L, u + 1))
                        for s in range(2):
                            z = ps(2 * (u % 2) + s, n)
                            act.activation(stay[:, u % 2, s, S - n:S], z, ACT.Sigmoid, scale=-SB_SCALE).then_inc(step.add(L), 1)
                            act.activation(take[:, u % 2, s, S - n:S], z, ACT.Sigmoid, scale=SB_SCALE).then_inc(sb_sig.sem, 1)
                    if u >= 1:
                        v = u - 1
                        n = (v % NT + 1) * P
                        act.wait_ge(sb_flip.sem, sb_flip.at(L, v + 1))
                        act.activation(wT[:, v % 2, 0, 0:n], ps(4, n), ACT.Copy).then_inc(sb_wT[0].sem, 1)
                        if v % NT == 0 and v:
                            pair_out(0, v // NT - 1, sb_o)
                pair_out(0, NPAIR - 1, sb_o)
                for t in range(NT + 1):
                    if t < NT:
                        act.wait_ge(up_done.sem, up_done.at(L, 2 * t + 1))
                        if t:
                            act.wait_ge(up_flip.sem, up_flip.at(L, 2 * t - 1))
                        act.activation(q_tok.rearrange("p a b -> p (a b)"), ps2(0, NH * QK), ACT.Copy,
                                       scale=MLA_SCALE).then_inc(q_out.sem, 1)
                        act.wait_ge(up_done.sem, up_done.at(L, 2 * t + 2))
                        if t:
                            act.wait_ge(up_flip.sem, up_flip.at(L, 2 * t))
                        kv = ps2(2, NH * 2 * HD).rearrange("p (a b) -> p a b", a=NH)
                        act.activation(k_tok[:, :, 0:HD], kv[:, :, 0:HD], ACT.Copy).then_inc(step.add(L), 1)
                        act.activation(v_att[:, t].rearrange("p (a b) -> p a b", a=NH), kv[:, :, HD:2 * HD],
                                       ACT.Copy).then_inc(k_out.sem, 1)
                    if t:
                        v = t - 1
                        act.wait_ge(up_flip.sem, up_flip.at(L, 2 * v + 1))
                        for g in range(2):
                            act.activation(qT[0:QK, 4 * g:4 * g + 4, v * P:(v + 1) * P],
                                           ps(4 + g, hi=QK).rearrange("p (a b) -> p a b", a=4), ACT.Copy).then_inc(qT_out.sem, 1)
                for u in range(UNITS + 1):
                    if u < UNITS:
                        n = (u % NT + 1) * P
                        for s in range(2):
                            act.wait_ge(ml_peak.sem, ml_peak.at(L, 2 * u + s + 1))
                            act.activation(prob[:, u % 2, s, 0:n], ps(2 * (u % 2) + s, n), ACT.Exp,
                                           bias=peak[:, u % 2, s:s + 1], accum_out=rsum[:, u % 2, s:s + 1]).then_inc(ml_exp.sem, 1)
                    if u >= 1:
                        v = u - 1
                        n = (v % NT + 1) * P
                        act.wait_ge(ml_flip.sem, ml_flip.at(L, v + 1))
                        act.activation(pTr[:, v % 2, 0, 0:n], ps(4, n), ACT.Copy).then_inc(ml_wT[0].sem, 1)
                        if v % NT == 0 and v:
                            pair_out(1, v // NT - 1, ml_o)
                pair_out(1, NPAIR - 1, ml_o)
                mean_squares(1, wo_out, 2)
                act.wait_ge(e_in.sem, e_in.at(L, 1))
                act.activation(gsc[:, :, 0:NG], gsc[:, :, 0:NG], ACT.Exp).then_inc(g_exp.sem, 1)
                act.wait_ge(e_in.sem, e_in.at(L, 2))
                act.activation(top_w[:, 1], top_w[:, 1], ACT.Exp).then_inc(e_exp.sem, 1)

                y_main = y_rows[0:MAIN].rearrange("(n p) d -> n p d", p=P)
                with act.Fori(0, PAIRS // 2) as i:
                    for b in range(2):
                        n = 2 * i + b
                        act.wait_ge(gu_done.sem, gu_done.at(L, n + 1))
                        act.activation(silu[b], ps(2 + b, DE), ACT.Silu).then_inc(silu_done.sem, 1)
                        act.wait_ge(dn_done.sem, dn_done.at(L, n + 1))
                        act.wait_ge(y_stored[b].sem, y_stored[b].at(L, 16 * i))
                        act.activation(y_out[b][:, HALF:D], ps(7), ACT.Copy).then_inc(y_act.sem, 1)
                        act.wait_ge(y_act.sem, y_act.at(L, n + 1))
                        act.wait_ge(y_dve.sem, y_dve.at(L, n + 1))
                        act.dma_start(y_main[n], y_out[b]).then_inc(y_stored[b].sem, 16)
                for b in range(2):
                    act.wait_ge(y_stored[b].sem, y_stored[b].at(L, 16 * PAIRS // 2))
                act.wait_ge(slots_ready.sem, slots_ready.at(L, 1))
                alone(act)
                so_far = act.value_load(xtra_i[0:1, 0:1], min_val=0, max_val=DEPTH * XTRA)
                n_xtra = act.value_load(xtra_i[0:1, 1:2], min_val=0, max_val=XTRA)
                y_over = y_rows[MAIN:].rearrange("(n p) d -> n p d", p=SLOT)
                with act.Fori(0, XTRA) as j:
                    with act.If(j < n_xtra):
                        act.wait_ge(x_gu, so_far + j + 1)
                        act.activation(silu[0][0:SLOT], ps(2, DE, hi=SLOT), ACT.Silu).then_inc(x_silu, 1)
                        act.wait_ge(x_y, so_far + j + 1)
                        act.dma_start(y_over[j], y_out[0][0:SLOT]).then_inc(x_store, 16)
                        act.wait_ge(x_store, 16 * (so_far + j + 1))
                        alone(act)
                    act.nop()
                act.sem_inc(x_over.sem, 1)
                for j in range(PC):
                    act.wait_ge(p_flip.sem, p_flip.at(L, j + 1))
                    act.activation(pT[:, j], ps(4 + j), ACT.Copy).then_inc(pT_ready.sem, 1)
                mean_squares(2, h_moe, 1)
                for k in range(2 * NT):
                    act.wait_ge(gate_done.sem, gate_done.at(L, k + 1))
                    if k >= 2:
                        act.wait_ge(ple_out.sem, ple_out.at(L, k - 1))
                    act.activation(gate_s[k % 2], ps(6 + k % 2), ACT.Sigmoid).then_inc(gate_out.sem, 1)
            assert step.n == STEPS_ACT
            for t in range(NT):
                act.wait_ge(ple_out.sem, ple_out.at(DEPTH, 2 * (t + 1) - 2 * NT))
                act.activation(junk[:], h[:, t], ACT.Square, scale=D ** -0.5, accum_out=ms[:, 12 + t:13 + t]).then_inc(fin_sq.sem, 1)
                act.wait_ge(fin_sq.sem, t + 1)

        @block.vector
        def _(dve):
            step = Steps(dve, dve_step)
            rstep = nc.alloc_semaphore("rstep")
            rn = [0]

            def link(ins):
                rn[0] += 1
                ins.then_inc(rstep, 1)
                dve.wait_ge(rstep, rn[0])

            dve.sem_inc(y_dve.sem, 1)
            dve.wait_ge(loaded.sem, 32)
            dve.wait_ge(const_ready.sem, 1)
            NF = ROPE // 2
            link(dve.tensor_copy(pos_f[:], pos_i[:]))
            link(dve.tensor_tensor(ang[:], pos_f[:].unsqueeze(2).to_broadcast([P, NT, NF]),
                                   inv_freq[:].unsqueeze(1).to_broadcast([P, NT, NF]), ALU.mult))
            two_pi = 2 * np.pi
            parts, left = [], two_pi
            for bits in (5, 9, 9):
                scale = 2.0 ** (bits - 1 - np.floor(np.log2(abs(left))))
                parts.append(float(np.round(left * scale) / scale))
                left -= parts[-1]
            parts.append(float(np.float32(left)))
            for whole, arg, quarter in ((turn, red, 0.0), (cos, turn, 0.25)):
                link(dve.tensor_scalar(whole[:], ang[:], float(1 / two_pi), quarter, ALU.mult, ALU.add))
                link(dve.tensor_scalar(whole[:], whole[:], ROUND, None, ALU.add))
                link(dve.tensor_scalar(whole[:], whole[:], ROUND, None, ALU.subtract))
                source = ang
                for c in parts:
                    link(dve.scalar_tensor_tensor(arg[:], whole[:], -c, source[:], ALU.mult, ALU.add))
                    source = arg
                if quarter:
                    link(dve.tensor_scalar(arg[:], arg[:], float(np.pi / 2), None, ALU.add))
                dve.tensor_scalar(arg[:], arg[:], 3.1415925, -3.1415925, ALU.min, ALU.max).then_inc(rope_ready.sem, 1)
                dve.wait_ge(rope_ready.sem, 1 if not quarter else 2)
            dve.wait_ge(rope_ready.sem, 4)
            dve.sem_inc(ple_out.sem, 2 * NT)

            with dve.Fori(0, DEPTH) as L:
                step.n = 0

                def norm(stage):
                    for t in range(NT + 1):
                        n = stage * NT + t
                        if t < NT:
                            dve.wait_ge(rooted.sem, rooted.at(L, n + 1))
                            if stage == 1 and t >= 2:
                                dve.wait_ge(xn_stored[t % 2].sem, xn_stored[t % 2].at(L, 16 * (t // 2)))
                            dve.tensor_scalar(xn[t % 2].rearrange("p (c q) -> p q c", c=DC),
                                              h[:, t].rearrange("p (q c) -> p q c", c=DC),
                                              rstd[:, n:n + 1], None, ALU.mult).then_inc(xn_ready.sem, 1)
                        if t:
                            dve.wait_ge(flipped.sem, flipped.at(L, n))
                            v = t - 1
                            for g in range(2):
                                gain = g_norm[:, stage, L, 4 * g:4 * g + 4]
                                dve.tensor_tensor(xT[:, 4 * g:4 * g + 4, v * P:(v + 1) * P],
                                                  ps(2 * (v % 2) + g).rearrange("p (a b) -> p a b", a=4),
                                                  gain.unsqueeze(2).to_broadcast([P, 4, P]), ALU.mult).then_inc(xT_ready.sem, 1)

                def rope(x1, x2, t, heads, to1, to2, done):
                    c = cos[:, t].unsqueeze(1).to_broadcast([P, heads, NF])
                    s = sin[:, t].unsqueeze(1).to_broadcast([P, heads, NF])
                    for k, (x, f) in enumerate(((x1, c), (x2, s), (x2, c), (x1, s))):
                        dve.tensor_tensor(rope_t[:, k, 0:heads], x, f, ALU.mult).then_inc(step.add(L), 1)
                    step.wait(L)
                    dve.tensor_tensor(to1, rope_t[:, 0, 0:heads], rope_t[:, 1, 0:heads], ALU.subtract).then_inc(step.add(L), 1)
                    dve.tensor_tensor(to2, rope_t[:, 2, 0:heads], rope_t[:, 3, 0:heads], ALU.add).then_inc(done.sem, 1)


                dve.wait_ge(gains_in.sem, 16 * (3 + 6 * DEPTH))
                norm(0)
                for k in range(NPAIR):
                    m = 2 * k + 1
                    dve.wait_ge(qk_done.sem, qk_done.at(L, m + 1))
                    to = qT_sb[:, m] if m < NPAIR else kT_sb[:, m - NPAIR]
                    dve.tensor_copy(to, ps(4 + m % 4)).then_inc(qk_dve.sem, 1)
                for t in range(NT + 1):
                    if t < NT:
                        dve.wait_ge(vl_done.sem, vl_done.at(L, t + 1))
                        dve.tensor_copy(lat[:, t], ps2(3 * (t % 2), LAT)).then_inc(lat_out.sem, 1)
                    if t:
                        v = t - 1
                        dve.wait_ge(lat_root.sem, lat_root.at(L, v + 1))
                        dve.tensor_scalar(lat[:, v, 0:QR], lat[:, v, 0:QR], rstd_lat[:, v, 0:1], None, ALU.mult).then_inc(step.add(L), 1)
                        dve.tensor_scalar(lat[:, v, QR:QR + KVR], lat[:, v, QR:QR + KVR], rstd_lat[:, v, 1:2], None,
                                          ALU.mult).then_inc(step.add(L), 1)
                        dve.wait_ge(lat_out.sem, lat_out.at(L, v + 1))
                        if v:
                            dve.wait_ge(lat_ready.sem, lat_ready.at(L, v))
                        at = QR + KVR
                        rope(lat[:, v, at:at + NF].unsqueeze(1), lat[:, v, at + NF:at + ROPE].unsqueeze(1), v, 1,
                             k_rot[:, v:v + 1, 0:NF], k_rot[:, v:v + 1, NF:ROPE], lat_ready)
                dve.wait_ge(lat_flip.sem, lat_flip.at(L, 1))
                for j in range(KVC):
                    to = dve.tensor_scalar(ckvT[:, j], ps(6 + j), g_lat[:, L, QC + j:QC + j + 1], None, ALU.mult)
                to.then_inc(ckvT_ready.sem, 1)
                for u in range(UNITS + 1):
                    if u < UNITS:
                        n = (u % NT + 1) * P
                        for s in range(2):
                            dve.wait_ge(sb_sig.sem, sb_sig.at(L, 2 * u + s + 1))
                            run = stay[:, u % 2, s, S - n:S][:, ::-1]
                            dve.tensor_tensor_scan(run, run, ones[:, 0:1].to_broadcast([P, n]), 1.0, ALU.mult,
                                                   ALU.mult).then_inc(sb_scan.sem, 1)
                    if u:
                        v = u - 1
                        n = (v % NT + 1) * P
                        dve.wait_ge(sb_flip.sem, sb_flip.at(L, v + 1))
                        dve.tensor_copy(wT[:, v % 2, 1, 0:n], ps(5, n)).then_inc(sb_wT[1].sem, 1)
                for t in range(NT + 1):
                    if t < NT:
                        if t == 1:
                            dve.wait_ge(o_ms.sem, o_ms.at(L, 1))
                            dve.tensor_scalar(ms_o[:, 0], ps(7, NT), 1.0 / SBW, None, ALU.mult).then_inc(o_ms_out.sem, 1)
                        dve.wait_ge(q_out.sem, q_out.at(L, t + 1))
                        if t:
                            dve.wait_ge(q_rope.sem, q_rope.at(L, t))
                        else:
                            dve.wait_ge(lat_ready.sem, lat_ready.at(L, NT))
                        rope(q_tok[:, :, HD:HD + NF], q_tok[:, :, HD + NF:QK], t, NH,
                             q_tok[:, :, HD:HD + NF], q_tok[:, :, HD + NF:QK], q_rope)
                        dve.wait_ge(k_out.sem, k_out.at(L, t + 1))
                        dve.tensor_copy(k_tok[:, :, HD:QK], k_rot[:, t].unsqueeze(1).to_broadcast([P, NH, ROPE])
                                        ).then_inc(k_rope.sem, 1)
                    if t:
                        v = t - 1
                        dve.wait_ge(up_flip.sem, up_flip.at(L, 2 * v + 2))
                        for g in range(2):
                            dve.tensor_copy(kT[0:QK, 4 * g:4 * g + 4, v * P:(v + 1) * P],
                                            ps(6 + g, hi=QK).rearrange("p (a b) -> p a b", a=4)).then_inc(kT_out.sem, 1)
                for u in range(UNITS + 1):
                    if u < UNITS:
                        n = (u % NT + 1) * P
                        dve.wait_ge(ml_z.sem, ml_z.at(L, u + 1))
                        for s in range(2):
                            dve.tensor_reduce(peak[:, u % 2, s:s + 1], ps(2 * (u % 2) + s, n), axis=AX.X, op=ALU.max,
                                              negate=True).then_inc(ml_peak.sem, 1)
                    if u:
                        v = u - 1
                        n = (v % NT + 1) * P
                        dve.wait_ge(ml_exp.sem, ml_exp.at(L, 2 * v + 2))
                        dve.reciprocal(rinv[:, v % 2], rsum[:, v % 2]).then_inc(step.add(L), 1)
                        step.wait(L)
                        for s in range(2):
                            dve.tensor_scalar(prob[:, v % 2, s, 0:n], prob[:, v % 2, s, 0:n], rinv[:, v % 2, s:s + 1], None,
                                              ALU.mult).then_inc(ml_w.sem, 1)
                        dve.wait_ge(ml_flip.sem, ml_flip.at(L, v + 1))
                        dve.tensor_copy(pTr[:, v % 2, 1, 0:n], ps(5, n)).then_inc(ml_wT[1].sem, 1)
                for k in range(2 * NT):
                    t, half = k // 2, k % 2
                    if k == 2:
                        dve.wait_ge(o_root.sem, o_root.at(L, 2))
                    part = h[:, t, half * HALF:(half + 1) * HALF]
                    b = 4 * (t % 2) + 2 * half
                    dve.wait_ge(wo_done.sem, wo_done.at(L, k + 1))
                    if k == 0:
                        dve.wait_ge(o_ms.sem, o_ms.at(L, 2))
                        dve.tensor_scalar(ms_o[:, 1], ps(4, NT), 1.0 / SBW, None, ALU.mult).then_inc(o_ms_out.sem, 1)
                        dve.wait_ge(o_root.sem, o_root.at(L, 2))
                    dve.scalar_tensor_tensor(part, ps(b), rstd_o[:, 0, t:t + 1], part, ALU.mult, ALU.add).then_inc(step.add(L), 1)
                    step.wait(L)
                    dve.scalar_tensor_tensor(part, ps(b + 1), rstd_o[:, 1, t:t + 1], part, ALU.mult, ALU.add).then_inc(wo_out.sem, 1)
                norm(1)

                def do(ins):
                    ins.then_inc(step.add(L), 1)
                    step.wait(L)

                four = [P, NT, NE]
                e_bc = expert_no[:].unsqueeze(1).to_broadcast(four)
                dve.wait_ge(r_done.sem, r_done.at(L, NT))
                dve.tensor_tensor(logit, ps(4, NT * NR).rearrange("p (a b) -> p a b", a=NT),
                                  b_r[:, L].unsqueeze(1).to_broadcast([P, NT, NR]), ALU.add).then_inc(r_out.sem, 1)
                do(dve.memset(g8, -BIG))
                dve.wait_ge(r_out.sem, r_out.at(L, 1))
                do(dve.tensor_copy(g8[:, :, 0:NG], logit[:, :, 0:NG]))
                for t in range(NT):
                    alone(dve)
                    dve.max(best8[:, t], g8[:, t]).then_inc(step.add(L), 1)
                step.wait(L)
                for t in range(NT):
                    alone(dve)
                    dve.max_index(g_i[:, t], best8[:, t], g8[:, t]).then_inc(step.add(L), 1)
                dve.tensor_tensor(gsc[:, :, 0:NG], logit[:, :, 0:NG], best8[:, :, 0:1].to_broadcast([P, NT, NG]),
                                  ALU.subtract).then_inc(e_in.sem, 1)
                step.wait(L)
                do(dve.tensor_copy(g_f[:], g_i[:, :, 0]))
                do(dve.tensor_tensor(gsc[:, :, NG:2 * NG], expert_no[:, 0:NG].unsqueeze(1).to_broadcast([P, NT, NG]),
                                     g_f[:].unsqueeze(2).to_broadcast([P, NT, NG]), ALU.is_equal))
                group = gsc[:, :, NG:2 * NG].unsqueeze(3).to_broadcast([P, NT, NG, EG])
                by_group = rtmp.rearrange("p t (g e) -> p t g e", g=NG)
                do(dve.tensor_tensor(by_group, logit[:, :, NG:NR].rearrange("p t (g e) -> p t g e", g=NG), group, ALU.mult))
                do(dve.tensor_scalar(gsc[:, :, NG:2 * NG], gsc[:, :, NG:2 * NG], BIG, -BIG, ALU.mult, ALU.add))
                do(dve.tensor_tensor(by_group, by_group, group, ALU.add))
                dve.wait_ge(e_in.sem, e_in.at(L, 1))
                for t in range(NT):
                    alone(dve)
                    dve.max(best8[:, t], rtmp[:, t]).then_inc(step.add(L), 1)
                step.wait(L)
                for t in range(NT):
                    alone(dve)
                    dve.max_index(best_i[:, t], best8[:, t], rtmp[:, t]).then_inc(step.add(L), 1)
                step.wait(L)
                do(dve.tensor_copy(best_f[:], best_i[:, :, 0:2]))
                for a in range(2):
                    dve.tensor_tensor(chosen[:, a], e_bc, best_f[:, :, a:a + 1].to_broadcast(four), ALU.is_equal).then_inc(step.add(L), 1)
                step.wait(L)
                dve.tensor_tensor(memb_b[:], chosen[:, 0], chosen[:, 1], ALU.add).then_inc(memb_ready.sem, 1)
                dve.tensor_tensor(top_w[:, 1], best8[:, :, 1], best8[:, :, 0], ALU.subtract).then_inc(e_in.sem, 1)
                dve.wait_ge(g_exp.sem, g_exp.at(L, 1))
                do(dve.tensor_reduce(gp[:], gsc[:, :, 0:NG], axis=AX.X, op=ALU.add))
                do(dve.reciprocal(gp[:], gp[:]))
                dve.wait_ge(e_exp.sem, e_exp.at(L, 1))
                do(dve.tensor_scalar(top_w[:, 0], top_w[:, 1], 1.0, None, ALU.add))
                do(dve.reciprocal(top_w[:, 0], top_w[:, 0]))
                do(dve.tensor_tensor(top_w[:, 0], top_w[:, 0], gp[:], ALU.mult))
                do(dve.tensor_tensor(top_w[:, 1], top_w[:, 1], top_w[:, 0], ALU.mult))
                dve.wait_ge(rank_done.sem, rank_done.at(L, 1))
                do(dve.tensor_copy(rank, ps(5, NT * NE).rearrange("p (a b) -> p a b", a=NT)))
                for a in range(2):
                    do(dve.tensor_tensor(over, chosen[:, a], rank, ALU.mult))
                    do(dve.tensor_reduce(rank_f[:, a], over, axis=AX.X, op=ALU.add))
                    dve.tensor_tensor(sel_tok[:, a * NT:(a + 1) * NT], chosen[:, a], tok_no[:].unsqueeze(2).to_broadcast(four),
                                      ALU.mult).then_inc(step.add(L), 1)
                step.wait(L)
                dve.tensor_tensor(sel_rank, slot_no[:].unsqueeze(1).to_broadcast([P, 2 * NT, P]),
                                  rank_f[:].rearrange("p a t -> p (a t)").unsqueeze(2).to_broadcast([P, 2 * NT, P]),
                                  ALU.is_equal).then_inc(sel_ready.sem, 1)
                dve.wait_ge(tok_done.sem, tok_done.at(L, 1))
                do(dve.tensor_copy(tok_i[0:SLOT, :], ps(6, NE, hi=SLOT)[:, 0:NE:2]))
                dve.tensor_copy(tok_i[SLOT:P, :], ps(6, NE, lo=SLOT)[:, 1:NE:2]).then_inc(tok_ready.sem, 1)
                do(dve.tensor_tensor(steps7, ps(5, NE, off=NT * NE).unsqueeze(2).to_broadcast([P, NE, 7]),
                                     thresh[:].unsqueeze(1).to_broadcast([P, NE, 7]), ALU.is_gt))
                do(dve.tensor_reduce(extra, steps7, axis=AX.X, op=ALU.add))
                do(dve.tensor_tensor_scan(extra_sum, extra, ones[:, 0:1].to_broadcast([P, NE]), 0.0, ALU.add, ALU.mult))
                do(dve.tensor_tensor(xtra_f[:, 0:1], xtra_f[:, 0:1], xtra_f[:, 1:2], ALU.add))
                do(dve.tensor_copy(xtra_f[:, 1:2], extra_sum[:, NE - 1:NE]))
                do(dve.tensor_tensor(steps15, extra_sum.unsqueeze(1).to_broadcast([P, 16, NE]),
                                     xtra_no[:].unsqueeze(2).to_broadcast([P, 16, NE]), ALU.is_le))
                do(dve.tensor_reduce(xtra_f[:, 2:18], steps15, axis=AX.X, op=ALU.add))
                do(dve.tensor_scalar(xtra_f[:, 2:18], xtra_f[:, 2:18], float(NE - 1), None, ALU.min))
                do(dve.tensor_copy(xtra_i[:], xtra_f[:]))
                do(dve.tensor_tensor(shift, extra_sum, extra, ALU.subtract))
                do(dve.tensor_tensor(shift, shift, expert_no[:], ALU.subtract))
                do(dve.tensor_scalar(shift, shift, float(SLOT), float(MAIN - SLOT), ALU.mult, ALU.add))
                do(dve.tensor_scalar(over, rank, float(SLOT), None, ALU.is_ge))
                do(dve.tensor_tensor(over, over, shift.unsqueeze(1).to_broadcast(four), ALU.mult))
                do(dve.tensor_tensor(rtmp, rank, over, ALU.add))
                do(dve.scalar_tensor_tensor(rtmp, e_bc, float(SLOT), rtmp, ALU.mult, ALU.add))
                for a in range(2):
                    do(dve.tensor_tensor(over, chosen[:, a], rtmp, ALU.mult))
                    do(dve.tensor_reduce(slot_f[:, a], over, axis=AX.X, op=ALU.add))
                do(dve.tensor_scalar(slot_x[:], slot_f[:], float(-MAIN), None, ALU.add))
                dve.tensor_copy(slot_i[:], slot_f[:]).then_inc(slots_ready.sem, 1)

                def gained(n, b):
                    dve.wait_ge(g_flip.sem, g_flip.at(L, n + 1))
                    for g in range(2):
                        gain = g_norm[:, 1, L, 4 * g:4 * g + 4].unsqueeze(2).to_broadcast([P, 4, P])
                        dve.tensor_tensor(xgT[b][:, 4 * g:4 * g + 4], ps(g).rearrange("p (a b) -> p a b", a=4), gain,
                                          ALU.mult).then_inc(xgT_ready.sem, 1)

                def pair(n, i, b, more):
                    dve.wait_ge(silu_done.sem, silu_done.at(L, n + 1))
                    dve.tensor_tensor(hid[b].rearrange("p (j q) -> p q j", j=EC),
                                      silu[b].rearrange("p (q j) -> p q j", j=EC),
                                      ps(2 + b, DE, off=DE).rearrange("p (q j) -> p q j", j=EC), ALU.mult).then_inc(hid_ready.sem, 1)
                    if more:
                        gained(n + 1, 1 - b)
                    dve.wait_ge(hid_flip.sem, hid_flip.at(L, n + 1))
                    dve.tensor_copy(hidT[b], ps(5, EC * P).rearrange("p (a b) -> p a b", a=EC)).then_inc(hidT_ready.sem, 1)
                    dve.wait_ge(dn_done.sem, dn_done.at(L, n + 1))
                    dve.wait_ge(y_stored[b].sem, y_stored[b].at(L, 16 * i))
                    dve.tensor_copy(y_out[b][:, 0:HALF], ps(6)).then_inc(y_dve.sem, 1)

                gained(0, 0)
                with dve.Fori(0, PAIRS // 2 - 1) as i:
                    for b in range(2):
                        pair(2 * i + b, i, b, True)
                pair(PAIRS - 2, PAIRS // 2 - 1, 0, True)
                pair(PAIRS - 1, PAIRS // 2 - 1, 1, False)
                for b in range(2):
                    dve.wait_ge(y_stored[b].sem, y_stored[b].at(L, 16 * PAIRS // 2))
                alone(dve)
                so_far = dve.value_load(xtra_i[0:1, 0:1], min_val=0, max_val=DEPTH * XTRA)
                n_xtra = dve.value_load(xtra_i[0:1, 1:2], min_val=0, max_val=XTRA)
                with dve.Fori(0, XTRA) as j:
                    with dve.If(j < n_xtra):
                        dve.tensor_tensor(sel_x, slot_no[:, 0:SLOT].unsqueeze(1).to_broadcast([P, 2 * NT, SLOT]),
                                          slot_x[:].rearrange("p a t -> p (a t)").unsqueeze(2).to_broadcast([P, 2 * NT, SLOT]),
                                          ALU.is_equal).then_inc(x_sel, 1)
                        dve.wait_ge(x_sel, 2 * (so_far + j) + 1)
                        dve.tensor_scalar(slot_x[:], slot_x[:], float(-SLOT), None, ALU.add).then_inc(x_sel, 1)
                        dve.wait_ge(x_sel, 2 * (so_far + j) + 2)
                        dve.wait_ge(x_tok, so_far + j + 1)
                        dve.tensor_copy(tokx_i[0:SLOT, :], ps(4, 1, hi=SLOT)).then_inc(x_idx, 1)
                        dve.wait_ge(x_flip, so_far + j + 1)
                        dve.tensor_tensor(xgT[0][:, :, 0:SLOT], ps(0).rearrange("p (a b) -> p a b", a=DC),
                                          g_norm[:, 1, L].unsqueeze(2).to_broadcast([P, DC, SLOT]), ALU.mult).then_inc(x_T, 1)
                        dve.wait_ge(x_silu, so_far + j + 1)
                        dve.tensor_tensor(hid[0][0:SLOT].rearrange("p (j q) -> p q j", j=EC),
                                          silu[0][0:SLOT].rearrange("p (q j) -> p q j", j=EC),
                                          ps(2, DE, off=DE, hi=SLOT).rearrange("p (q j) -> p q j", j=EC), ALU.mult).then_inc(x_hid, 1)
                        dve.wait_ge(x_hflip, so_far + j + 1)
                        dve.tensor_copy(hidT[0][:, :, 0:SLOT], ps(5, EC * SLOT).rearrange("p (a b) -> p a b", a=EC)).then_inc(x_hT, 1)
                        dve.wait_ge(x_dn, so_far + j + 1)
                        dve.tensor_copy(y_out[0][0:SLOT], ps2(6, D)[0:SLOT]).then_inc(x_y, 1)
                    dve.nop()
                for t in range(NT):
                    dve.wait_ge(back_in[t % 2].sem, back_in[t % 2].at(L, 32 * (t // 2 + 1)))
                    dve.scalar_tensor_tensor(h[:, t], back[2 * (t % 2)], top_w[:, 0, t:t + 1], h[:, t], ALU.mult,
                                             ALU.add).then_inc(step.add(L), 1)
                    step.wait(L)
                    dve.scalar_tensor_tensor(h[:, t], back[2 * (t % 2) + 1], top_w[:, 1, t:t + 1], h[:, t], ALU.mult,
                                             ALU.add).then_inc(h_moe.sem, 1)
                norm(2)
                for k in range(2 * NT):
                    part = h[:, k // 2, (k % 2) * HALF:(k % 2 + 1) * HALF]
                    dve.wait_ge(gate_out.sem, gate_out.at(L, k + 1))
                    dve.wait_ge(pe_done.sem, pe_done.at(L, k + 1))
                    dve.tensor_tensor(gate_s[k % 2], gate_s[k % 2], ps(4 + k % 2), ALU.mult).then_inc(step.add(L), 1)
                    step.wait(L)
                    dve.tensor_tensor(part, part, gate_s[k % 2], ALU.add).then_inc(ple_out.sem, 1)
            assert step.n == STEPS_DVE
            dve.wait_ge(g_last_in.sem, 16)
            for t in range(NT):
                dve.wait_ge(fin_root.sem, t + 1)
                dve.scalar_tensor_tensor(h[:, t], h[:, t], rstd[:, 12 + t:13 + t], g_last, ALU.mult, ALU.mult).then_inc(fin_ready.sem, 1)

        @block.tensor
        def _(pe):
            pe.sem_inc(pe_done.sem, 1)
            pe.wait_ge(const_ready.sem, 1)

            with pe.Fori(0, DEPTH) as L:

                def norm(stage):
                    for t in range(NT):
                        n = stage * NT + t
                        pe.wait_ge(xn_ready.sem, xn_ready.at(L, n + 1))
                        if t >= 2:
                            pe.wait_ge(xT_ready.sem, xT_ready.at(L, 2 * (n - 1)))
                        for c in range(DC):
                            last = pe.transpose(ps(2 * (t % 2) + c // 4, P, off=(c % 4) * P), xn[t % 2][:, c * P:(c + 1) * P], ident[:])
                        last.then_inc(flipped.sem, 1)

                norm(0)
                pe.wait_ge(xT_ready.sem, xT_ready.at(L, 2 * NT))
                pe.wait_ge(w_in_in.sem, w_in_in.at(L, 2 * 16))
                pe.wait_ge(ple_out.sem, ple_out.at(L, 0))
                for m in range(2 * NPAIR):
                    if m >= 4:
                        freed = (qk_act, qk_dve)[m % 2]
                        pe.wait_ge(freed.sem, freed.at(L, (m - 4) // 2 + 1))
                    for c in range(DC):
                        last = pe.matmul(ps(4 + m % 4), w_qk[:, c, m * P:(m + 1) * P], xT[:, c], start=(c == 0), stop=(c == DC - 1))
                    last.then_inc(qk_done.sem, 1)
                for t in range(NT):
                    if t == 1:
                        pe.wait_ge(qk_act.sem, qk_act.at(L, 3))
                        pe.wait_ge(qk_dve.sem, qk_dve.at(L, 3))
                    if t >= 2:
                        pe.wait_ge(v_out.sem, v_out.at(L, t - 1))
                        pe.wait_ge(lat_out.sem, lat_out.at(L, t - 1))
                    b = 3 * (t % 2)
                    for to, lo, n in ((ps(b), SBW, 512), (ps(b + 1, LAT - 512), SBW + 512, LAT - 512), (ps(b + 2), 0, SBW)):
                        for c in range(DC):
                            last = pe.matmul(to, xT[:, c, t * P:(t + 1) * P], w_vl[:, c, lo:lo + n], start=(c == 0), stop=(c == DC - 1))
                    last.then_inc(vl_done.sem, 1)
                pe.wait_ge(v_out.sem, v_out.at(L, NT))
                pe.wait_ge(lat_out.sem, lat_out.at(L, NT))
                pe.wait_ge(qk_act.sem, qk_act.at(L, NPAIR))
                pe.wait_ge(qk_dve.sem, qk_dve.at(L, NPAIR))
                for t in range(NT):
                    pe.wait_ge(lat_ready.sem, lat_ready.at(L, t + 1))
                    for j in range(QC + KVC):
                        last = pe.transpose(ps(3 + j, P, off=t * P), lat[:, t, j * P:(j + 1) * P], ident[:])
                last.then_inc(lat_flip.sem, 1)

                def scores(u, q, k, depth, scale_mask, done):
                    m, qb = u // NT, u % NT
                    n = (qb + 1) * P
                    for s in range(2):
                        z = ps(2 * (u % 2) + s, n)
                        pe.matmul(z, q(m, s, qb), k(m, s, n), start=True, stop=False)
                        last = pe.matmul(ps(2 * (u % 2) + s, P, off=n - P), ident_b[:], scale_mask[:], start=False, stop=True)
                    last.then_inc(done.sem, 1)

                def flip(u, w, done):
                    for s in range(2):
                        for kb in range(u % NT + 1):
                            last = pe.transpose(ps(4 + s, P, off=kb * P), w(u, s, kb), ident[:])
                    last.then_inc(done.sem, 1)

                def outputs(u, w, done):
                    m, qb = u // NT, u % NT
                    for kb in range(qb + 1):
                        for s in range(2):
                            hd = 2 * m + s
                            last = pe.matmul(ps(6 + m % 2, P, off=qb * P, lo=HD * s, hi=HD * (s + 1)),
                                             v_att[:, kb, hd * HD:(hd + 1) * HD], w[:, u % 2, s, kb * P:(kb + 1) * P],
                                             start=(kb == 0), stop=(kb == qb), skip_group_check=True)
                    last.then_inc(done.sem, 1)

                def attention(q, k, depth, mask, kind, z_done, z_used, w_ready, flipped_, wT_ready, wT_, weights, o_done, before_t, before_o):
                    for u in range(2):
                        scores(u, q, k, depth, mask, z_done)
                    for u in range(UNITS):
                        pe.wait_ge(w_ready.sem, w_ready.at(L, 2 * u + 2))
                        if u:
                            for s in range(2):
                                pe.wait_ge(wT_ready[s].sem, wT_ready[s].at(L, u))
                        flip(u, weights, flipped_)
                        if u + 2 < UNITS:
                            pe.wait_ge(z_used.sem, z_used.at(L, 2 * u + 2))
                            scores(u + 2, q, k, depth, mask, z_done)
                        for s in range(2):
                            pe.wait_ge(wT_ready[s].sem, wT_ready[s].at(L, u + 1))
                        m = u // NT
                        if u % NT == 0 and m >= 2:
                            pe.wait_ge(o_sq.sem, o_sq.at(L, kind * NPAIR + m - 1))
                        outputs(u, wT_, o_done)

                pe.wait_ge(cqT_ready.sem, cqT_ready.at(L, 1))
                pe.wait_ge(ckvT_ready.sem, ckvT_ready.at(L, 1))
                attention(lambda m, s, qb: qT_sb[HD * s:HD * (s + 1), m, qb * P:(qb + 1) * P],
                          lambda m, s, n: kT_sb[HD * s:HD * (s + 1), m, 0:n], HD, sb_mask, 0, sb_z, sb_sig, sb_w, sb_flip,
                          sb_wT, wT, lambda u, s, kb: take[:, u % 2, s, S - (u % NT + 1) * P + kb * P:S - (u % NT + 1) * P + (kb + 1) * P],
                          sb_o, None, None)
                pe.wait_ge(w_up_in.sem, w_up_in.at(L, 2 * 16))
                pe.wait_ge(sb_sig.sem, sb_sig.at(L, 2 * UNITS))
                for t in range(NT + 1):
                    if t < NT:
                        if t:
                            pe.wait_ge(q_out.sem, q_out.at(L, t))
                        for lo, n in ((0, 512), (512, NH * QK - 512)):
                            for j in range(QC):
                                last = pe.matmul(ps(lo // 512, n), cqT[:, j, t * P:(t + 1) * P], w_uq[:, j, lo:lo + n],
                                                 start=(j == 0), stop=(j == QC - 1))
                        last.then_inc(up_done.sem, 1)
                        if t:
                            pe.wait_ge(k_out.sem, k_out.at(L, t))
                        for lo in (0, 512):
                            for j in range(KVC):
                                last = pe.matmul(ps(2 + lo // 512), ckvT[:, j, t * P:(t + 1) * P], w_ukv[:, j, lo:lo + 512],
                                                 start=(j == 0), stop=(j == KVC - 1))
                        last.then_inc(up_done.sem, 1)
                    if t == 0:
                        pe.wait_ge(o_sum.sem, o_sum.at(L, NPAIR))
                        for k in range(NT):
                            last = pe.matmul(ps(7, 1, off=k), o_total[0][:, k * P:(k + 1) * P], ones[:, 0:1], start=True, stop=True)
                        last.then_inc(o_ms.sem, 1)
                    else:
                        v = t - 1
                        pe.wait_ge(q_rope.sem, q_rope.at(L, v + 1))
                        if v:
                            pe.wait_ge(qT_out.sem, qT_out.at(L, 2 * v))
                        for hd in range(NH):
                            last = pe.transpose(ps(4 + hd // 4, P, off=(hd % 4) * P, hi=QK), q_tok[:, hd], ident[:])
                        last.then_inc(up_flip.sem, 1)
                        pe.wait_ge(k_rope.sem, k_rope.at(L, v + 1))
                        if v:
                            pe.wait_ge(kT_out.sem, kT_out.at(L, 2 * v))
                        else:
                            pe.wait_ge(o_ms_out.sem, o_ms_out.at(L, 1))
                        for hd in range(NH):
                            last = pe.transpose(ps(6 + hd // 4, P, off=(hd % 4) * P, hi=QK), k_tok[:, hd], ident[:])
                        last.then_inc(up_flip.sem, 1)
                pe.wait_ge(qT_out.sem, qT_out.at(L, 2 * NT))
                pe.wait_ge(kT_out.sem, kT_out.at(L, 2 * NT))
                attention(lambda m, s, qb: qT[0:QK, 2 * m + s, qb * P:(qb + 1) * P],
                          lambda m, s, n: kT[0:QK, 2 * m + s, 0:n], QK, mla_mask, 1, ml_z, ml_exp, ml_w, ml_flip,
                          ml_wT, pTr, lambda u, s, kb: prob[:, u % 2, s, kb * P:(kb + 1) * P], ml_o, None, None)
                pe.wait_ge(w_o_in.sem, w_o_in.at(L, 16))
                pe.wait_ge(o_sq.sem, o_sq.at(L, NPAIR))
                for t in range(NT):
                    if t == 1:
                        pe.wait_ge(o_sum.sem, o_sum.at(L, 2 * NPAIR))
                        for k in range(NT):
                            last = pe.matmul(ps(4, 1, off=k), o_total[1][:, k * P:(k + 1) * P], ones[:, 0:1], start=True, stop=True)
                        last.then_inc(o_ms.sem, 1)
                        pe.wait_ge(o_ms_out.sem, o_ms_out.at(L, 2))
                    if t >= 2:
                        pe.wait_ge(wo_out.sem, wo_out.at(L, 2 * (t - 1)))
                    for half in range(2):
                        for kind in range(2):
                            if kind == 1 and t == 0 and half == 0:
                                pe.wait_ge(o_sq.sem, o_sq.at(L, 2 * NPAIR))
                            for m in range(NPAIR):
                                c = kind * NPAIR + m
                                last = pe.matmul(ps(4 * (t % 2) + 2 * half + kind), oT[:, c, t * P:(t + 1) * P],
                                                 w_o[:, c, half * HALF:(half + 1) * HALF], start=(m == 0), stop=(m == NPAIR - 1))
                        last.then_inc(wo_done.sem, 1)
                pe.wait_ge(wo_out.sem, wo_out.at(L, 2 * (NT - 1)))
                norm(1)
                pe.wait_ge(wo_out.sem, wo_out.at(L, 2 * NT))
                pe.wait_ge(r_in.sem, r_in.at(L, 2 * 16))
                for t in range(NT):
                    pe.wait_ge(xT_ready.sem, xT_ready.at(L, 2 * NT + 2 * (t + 1)))
                    for c in range(DC):
                        last = pe.matmul(ps(4, NR, off=t * NR), xT[:, c, t * P:(t + 1) * P], w_r[:, c], start=(c == 0), stop=(c == DC - 1))
                    last.then_inc(r_done.sem, 1)
                pe.wait_ge(memb_ready.sem, memb_ready.at(L, 1))
                for t in range(NT + 1):
                    n = min(t, NT - 1)
                    for k in range(n + 1):
                        last = pe.matmul(ps(5, NE, off=t * NE), before_b[:] if k == t else ones_b[:], memb_b[:, k],
                                         start=(k == 0), stop=(k == n))
                last.then_inc(rank_done.sem, 1)
                pe.wait_ge(sel_ready.sem, sel_ready.at(L, 1))
                for k in range(2 * NT):
                    last = pe.matmul(ps(6, NE), sel_rank[:, k], sel_tok[:, k], start=(k == 0), stop=(k == 2 * NT - 1))
                last.then_inc(tok_done.sem, 1)

                def tokens(n, i, b):
                    pe.wait_ge(gathered[b].sem, gathered[b].at(L, 16 * (i + 1)))
                    for c in range(DC):
                        last = pe.transpose(ps(c // 4, P, off=(c % 4) * P), xg[b][:, c * P:(c + 1) * P], ident[:])
                    last.then_inc(g_flip.sem, 1)

                def pair(n, i, b, more):
                    pe.wait_ge(xgT_ready.sem, xgT_ready.at(L, 2 * n + 2))
                    pe.wait_ge(gu_in[b].sem, gu_in[b].at(L, 32 * (i + 1)))
                    for c in range(DC):
                        for e in range(2):
                            last = pe.matmul(ps(2 + b, lo=SLOT * e, hi=SLOT * (e + 1)), xgT[b][:, c, SLOT * e:SLOT * (e + 1)],
                                             w_gu[2 * b + e][:, :, c], start=(c == 0), stop=(c == DC - 1), skip_group_check=True)
                    last.then_inc(gu_done.sem, 1)
                    if more:
                        tokens(n + 1, i + b, 1 - b)
                    pe.wait_ge(hid_ready.sem, hid_ready.at(L, n + 1))
                    for j in range(EC):
                        last = pe.transpose(ps(5, P, off=j * P), hid[b][:, j * P:(j + 1) * P], ident[:])
                    last.then_inc(hid_flip.sem, 1)
                    pe.wait_ge(hidT_ready.sem, hidT_ready.at(L, n + 1))
                    pe.wait_ge(dn_in[b].sem, dn_in[b].at(L, 16 * (i + 1)))
                    pe.wait_ge(y_act.sem, y_act.at(L, n))
                    pe.wait_ge(y_dve.sem, y_dve.at(L, n))
                    for half in range(2):
                        for j in range(EC):
                            for e in range(2):
                                last = pe.matmul(ps(6 + half, lo=SLOT * e, hi=SLOT * (e + 1)), hidT[b][:, j, SLOT * e:SLOT * (e + 1)],
                                                 w_dn[2 * b + e][:, j, half * HALF:(half + 1) * HALF],
                                                 start=(j == 0), stop=(j == EC - 1), skip_group_check=True)
                    last.then_inc(dn_done.sem, 1)

                tokens(0, 0, 0)
                with pe.Fori(0, PAIRS // 2 - 1) as i:
                    for b in range(2):
                        pair(2 * i + b, i, b, True)
                pair(PAIRS - 2, PAIRS // 2 - 1, 0, True)
                pair(PAIRS - 1, PAIRS // 2 - 1, 1, False)
                pe.wait_ge(y_act.sem, y_act.at(L, PAIRS))
                pe.wait_ge(y_dve.sem, y_dve.at(L, PAIRS))
                pe.wait_ge(slots_ready.sem, slots_ready.at(L, 1))
                alone(pe)
                so_far = pe.value_load(xtra_i[0:1, 0:1], min_val=0, max_val=DEPTH * XTRA)
                n_xtra = pe.value_load(xtra_i[0:1, 1:2], min_val=0, max_val=XTRA)
                with pe.Fori(0, XTRA) as j:
                    with pe.If(j < n_xtra):
                        pe.wait_ge(x_sel, 2 * (so_far + j) + 1)
                        for k in range(2 * NT):
                            last = pe.matmul(ps(4, 1, hi=SLOT), sel_x[:, k], tok_no[:, k % NT:k % NT + 1], start=(k == 0), stop=(k == 2 * NT - 1))
                        last.then_inc(x_tok, 1)
                        pe.wait_ge(x_gather, 16 * (so_far + j + 1))
                        alone(pe)
                        for c in range(DC):
                            last = pe.transpose(ps(0, SLOT, off=c * SLOT), xg[0][0:SLOT, c * P:(c + 1) * P], ident[0:SLOT, 0:SLOT])
                        last.then_inc(x_flip, 1)
                        pe.wait_ge(x_T, so_far + j + 1)
                        pe.wait_ge(x_w, 48 * (so_far + j + 1))
                        for c in range(DC):
                            last = pe.matmul(ps(2, hi=SLOT), xgT[0][:, c, 0:SLOT], w_gu[0][:, :, c], start=(c == 0), stop=(c == DC - 1))
                        last.then_inc(x_gu, 1)
                        pe.wait_ge(x_hid, so_far + j + 1)
                        alone(pe)
                        for k in range(EC):
                            last = pe.transpose(ps(5, SLOT, off=k * SLOT), hid[0][0:SLOT, k * P:(k + 1) * P], ident[0:SLOT, 0:SLOT])
                        last.then_inc(x_hflip, 1)
                        pe.wait_ge(x_hT, so_far + j + 1)
                        for half in range(2):
                            for k in range(EC):
                                last = pe.matmul(ps(6 + half, hi=SLOT), hidT[0][:, k, 0:SLOT], w_dn[0][:, k, half * HALF:(half + 1) * HALF],
                                                 start=(k == 0), stop=(k == EC - 1))
                        last.then_inc(x_dn, 1)
                    pe.nop()
                pe.wait_ge(x_over.sem, x_over.at(L, 1))
                pe.wait_ge(w_e_in.sem, w_e_in.at(L, 2 * 16))
                for j in range(PC):
                    for t in range(NT):
                        last = pe.transpose(ps(4 + j, P, off=t * P), p_tok[:, t, j:PE_IN:PC], ident[:])
                    last.then_inc(p_flip.sem, 1)
                norm(2)
                pe.wait_ge(w_g_in.sem, w_g_in.at(L, 16))
                pe.wait_ge(pT_ready.sem, pT_ready.at(L, PC))
                for k in range(2 * NT):
                    t, half = k // 2, k % 2
                    cols = slice(half * HALF, (half + 1) * HALF)
                    if half == 0:
                        pe.wait_ge(xT_ready.sem, xT_ready.at(L, 4 * NT + 2 * (t + 1)))
                    if k >= 2:
                        pe.wait_ge(gate_out.sem, gate_out.at(L, k - 1))
                    for c in range(DC):
                        last = pe.matmul(ps(6 + k % 2), xT[:, c, t * P:(t + 1) * P], w_g[:, c, cols], start=(c == 0), stop=(c == DC - 1))
                    last.then_inc(gate_done.sem, 1)
                    if k >= 2:
                        pe.wait_ge(ple_out.sem, ple_out.at(L, k - 1))
                    for j in range(PC):
                        last = pe.matmul(ps(4 + k % 2), pT[:, j, t * P:(t + 1) * P], w_e[:, j, cols], start=(j == 0), stop=(j == PC - 1))
                    last.then_inc(pe_done.sem, 1)


_INS = ["x", "p", "positions", "g_mix", "w_in", "g_cq", "w_uq", "g_ckv", "w_ukv", "g_osb", "g_omla", "w_out", "g_moe",
        "w_rg", "b_rg", "w_re", "b_re", "w_gate", "w_up", "w_down", "g_ple", "w_pg", "w_pe", "g_final"]


def kernel(**inputs):
    import numpy as np
    import concourse.bacc as bacc
    from concourse import mybir
    from concourse.bass_utils import run_bass_kernel_spmd

    nc = bacc.Bacc("TRN2", target_bir_lowering=False, num_devices=1)
    arrays, io = {}, {}
    for name in _INS:
        a = np.ascontiguousarray(inputs[name])
        arrays[f"in_{name}"] = a
        io[name] = nc.dram_tensor(f"in_{name}", a.shape, mybir.dt.from_np(a.dtype), kind="ExternalInput").ap()
    shape = inputs["x"].shape
    out = nc.dram_tensor("out_trunk", shape, mybir.dt.float32, kind="ExternalOutput").ap()
    _program(nc, io, out)
    r = run_bass_kernel_spmd(nc, [arrays], core_ids=[0])
    return r.results[0]["out_trunk"]
```

```python
def _program(nc, io, out):
    import numpy as np
    import concourse.bass as bass
    from concourse import mybir

    fp32, bf16, i32, u32 = mybir.dt.float32, mybir.dt.bfloat16, mybir.dt.int32, mybir.dt.uint32
    fp32r = mybir.dt.float32r
    ALU, ACT, AX = mybir.AluOpType, mybir.ActivationFunctionType, mybir.AxisListType

    P = 128
    DEPTH, D = io["g_mix"].shape
    S = io["x"].shape[1]
    NT = S // P
    DC = D // P
    HALF = D // 2
    NH, HD = 8, 64
    NPAIR = NH // 2
    QR, KVR, ROPE = io["g_cq"].shape[1], io["g_ckv"].shape[1], 32
    QC, KVC = QR // P, KVR // P
    QK = HD + ROPE
    SBW = NH * HD
    IN = io["w_in"].shape[2]
    LAT = IN - 3 * SBW
    NG, NE = io["w_rg"].shape[2], io["w_re"].shape[2]
    NR = NG + NE
    EG = NE // NG
    DE = io["w_gate"].shape[3]
    EC = DE // P
    SLOT = 64
    PAIRS = NE // 2
    MAIN = NE * SLOT
    XTRA = 2 * S // (SLOT + 1)
    PE_IN = io["p"].shape[3]
    PC = PE_IN // P
    CHUNK = 64
    EPS = 1e-6
    BIG = 1e30
    ROUND = 1.5 * 2.0 ** 23
    SB_SCALE, MLA_SCALE = HD ** -0.5, QK ** -0.5

    y_rows = nc.dram_tensor("y_rows", [2 * S, D], fp32, kind="Internal").ap()

    W_IN = DC * IN
    WORDS, SPLIT = 50560, 33024
    WORDS_AT = -(-nc.sbuf_base // 32) * 32
    low = nc.alloc_sbuf_tensor("low", [P, SPLIT], fp32)
    high = nc.alloc_sbuf_tensor("high", [P, WORDS - SPLIT], fp32)

    def cut(at, *shape):
        n = int(np.prod(shape))
        v = low[:, at:at + n] if at < SPLIT else high[:, at - SPLIT:at - SPLIT + n]
        if len(shape) == 2:
            v = v.rearrange("p (a b) -> p a b", a=shape[0])
        if len(shape) == 3:
            v = v.rearrange("p (a b c) -> p a b c", a=shape[0], b=shape[1])
        return v

    def rounded(name, at, *shape):
        return nc.alloc_sbuf_tensor_at(name, [P] + list(shape), fp32r, offset=WORDS_AT + 4 * at)[:]

    h = cut(0, NT, D)
    ARENA = NT * D
    w_qk = cut(ARENA, DC, 2 * SBW)
    w_vl = cut(ARENA + DC * 2 * SBW, DC, IN - 2 * SBW)
    EXPERT = 2 * DC * DE + EC * D
    W_UP = QC * NH * QK + KVC * NH * 2 * HD
    SLOT_AT = [ARENA + W_UP + DC * D + e * EXPERT for e in range(2)] + [ARENA + e * EXPERT for e in range(2)]
    w_gu = [cut(at, 2, DC, DE) for at in SLOT_AT]
    w_dn = [cut(at + 2 * DC * DE, EC, D) for at in SLOT_AT]
    w_pair = [cut(SLOT_AT[2 * b], 2, EXPERT) for b in range(2)]
    w_uq = cut(ARENA, QC, NH * QK)
    w_ukv = cut(ARENA + QC * NH * QK, KVC, NH * 2 * HD)
    w_o = cut(ARENA + W_UP, 2 * NPAIR, D)
    XT = ARENA + W_UP + DC * D + 2 * EXPERT
    w_g = cut(ARENA + W_IN, DC - 1, D)
    xT = cut(XT, DC, S)
    kT = cut(XT, NH, S)
    XN = XT + DC * S
    assert XN == SPLIT
    xn = [cut(XN + b * D, D) for b in range(2)]
    q_tok = cut(XN, NH, QK)
    k_tok = cut(XN + D, NH, QK)
    LATENT = XN + 2 * D
    lat = cut(LATENT, NT, LAT)
    ATT = LATENT + NT * LAT
    qT_sb = cut(ATT, NPAIR, S)
    kT_sb = cut(ATT + NPAIR * S, NPAIR, S)
    qT = cut(ATT, NH, S)
    v_att = cut(ATT + 2 * NPAIR * S, NT, SBW)
    oT = cut(ATT + 2 * NPAIR * S + NT * SBW, 2 * NPAIR, S)
    cqT = cut(ATT + 2 * NPAIR * S + NT * SBW + 2 * NPAIR * S, QC, S)
    ckvT = cut(ATT + 2 * NPAIR * S + NT * SBW + 2 * NPAIR * S + QC * S, KVC, S)
    PART = ARENA + W_IN
    x_tile = [cut(PART + b * D, DC, P) for b in range(2)]
    x_hi = rounded("x_hi", XT, DC, S)
    x_lo = rounded("x_lo", ATT + 2 * NPAIR * S + NT * SBW, DC, S)
    w_hi = [rounded(f"w_hi{b}", PART + 2 * D + b * 512, 512) for b in range(4)]
    w_lo = [rounded(f"w_lo{b}", PART + 4 * D + b * 512, 512) for b in range(4)]
    rope_k = cut(PART + 6 * D, 4, 1, ROPE // 2)
    QK_UNITS = 2 * 2 * NPAIR
    GROUPS = ((SBW, LAT // 2), (SBW + LAT // 2, LAT // 2), (0, SBW))
    IN_UNITS = QK_UNITS + len(GROUPS) * DC
    rope_t = cut(ATT + 2 * NPAIR * S + NT * SBW + (2 * NPAIR - 1) * S, 4, NH, ROPE // 2)
    take = cut(XT, 2, 2, S)
    wT = cut(XT + 4 * S, 2, 2, S)
    stay = cut(XN, 2, 2, S + 2)
    prob = cut(XN, 2, 2, S)
    pTr = cut(XN + 4 * S, 2, 2, S)
    o_square = [cut(XN + 4 * (S + 2), 2, S), cqT[:, 0:2, :]]
    o_total = [cut(XN + 4 * (S + 2) + 2 * S, S), cqT[:, 2, :]]
    x_parts = rounded("x_parts", LATENT, 2, NT, D)
    xgT = [cut(LATENT + at * D, DC, 2 * P) for at in (8, 12)]
    y_out = [cut(LATENT + (10 + b) * D, D) for b in range(2)]
    w_e = cut(SLOT_AT[0], PC, D)
    p_tok = cut(SLOT_AT[0] + PC * D, NT, PE_IN)
    pT = cut(SLOT_AT[0] + PC * D, PC, S)
    back = [cut(LATENT + 2 * b * D, 2, D) for b in range(3)]
    w_g_last = cut(LATENT + 6 * D, D)
    emb = cut(LATENT + 8 * D, NT, D)
    gate_s = [cut(LATENT + 12 * D + b * HALF, HALF) for b in range(2)]
    silu = [cut(XN + b * 3 * DE, DE) for b in range(2)]
    hid = [cut(XN + b * 3 * DE + DE, DE) for b in range(2)]
    hidT = [cut(XN + b * 3 * DE + 2 * DE, EC, P) for b in range(2)]
    sel = rounded("sel", XT, NT, 2 * P)
    sel_half = cut(XT + 2 * NT * P, NT, P)
    sel_other = cut(XT + 3 * NT * P, NT, P)
    sel_x = cut(XT + 6 * NT * P, 2 * NT, SLOT)
    R0 = XT + 4 * NT * P
    steps7 = cut(R0, NE, 7)
    steps15 = cut(R0 + 256, 16, NE)
    R1 = R0 + 768
    sel_rank = cut(LATENT + 8 * D, 2 * NT, P)
    sel_tok = cut(LATENT + 9 * D, 2 * NT, NE)
    logit = cut(R1, NT, NR)
    g8 = cut(R1 + 144, NT, 8)
    rank = cut(R1 + 176, NT, NE)
    rtmp = cut(R1 + 304, NT, NE)
    over = cut(R1 + 432, NT, NE)
    best8 = cut(R1 + 560, NT, 8)
    extra = cut(R1 + 592, NE)
    extra_sum = cut(R1 + 624, NE)
    shift = cut(R1 + 656, NE)
    gsc = cut(R1 + 688, NT, 8)
    row_g = cut(R1 + 720, PAIRS + 1)
    g_last = cut(XT, D)

    def sb(name, shape, dt=fp32):
        return nc.alloc_sbuf_tensor(name, [P] + list(shape), dt)

    ident, ones = sb("ident", [P]), sb("ones", [P])
    ident_b, ones_b, before_b = sb("ident_b", [P], bf16), sb("ones_b", [P], bf16), sb("before_b", [P], bf16)
    sb_mask, mla_mask = sb("sb_mask", [P], bf16), sb("mla_mask", [P], bf16)
    junk = sb("junk", [D], bf16)
    cos, sin = sb("cos", [NT, ROPE // 2]), sb("sin", [NT, ROPE // 2])
    pair_slot, expert_no = sb("pair_slot", [P]), sb("expert_no", [NE])
    row_no = sb("row_no", [2, NT])
    thresh, xtra_no = sb("thresh", [7]), sb("xtra_no", [16])
    minus_half = sb("minus_half", [8])
    g_norm = sb("g_norm", [3, DEPTH, DC])
    g_lat = sb("g_lat", [DEPTH, QC + KVC])
    g_o = sb("g_o", [DEPTH, 2 * NPAIR])
    b_r = sb("b_r", [DEPTH, NR])
    w_r = sb("w_r", [DC, NR])
    pos_i, pos_f = sb("pos_i", [NT], i32), sb("pos_f", [NT])
    inv_freq = sb("inv_freq", [ROPE // 2])
    ang, turn, red = (cut(XT + k * NT * ROPE // 2, NT, ROPE // 2) for k in range(3))
    k_rot = sb("k_rot", [NT, ROPE])
    ms, rstd = sb("ms", [16]), sb("rstd", [16])
    ms_lat, rstd_lat = sb("ms_lat", [NT, 2]), sb("rstd_lat", [NT, 2])
    ms_o, rstd_o = sb("ms_o", [2, NT]), sb("rstd_o", [2, NT])
    peak, rsum, rinv = sb("peak", [2, 2]), sb("rsum", [2, 2]), sb("rinv", [2, 2])
    memb_b = sb("memb_b", [NT, NE], bf16)
    best_i, g_i = sb("best_i", [NT, 8], u32), sb("g_i", [NT, 8], u32)
    best_f, g_f = sb("best_f", [NT, 2]), sb("g_f", [NT])
    chosen = sb("chosen", [2, NT, NE])
    rank_f = sb("rank_f", [2, NT])
    gp, top_w = sb("gp", [NT]), sb("top_w", [2, NT])
    slot_f = sb("slot_f", [2, NT])
    slot_x = sb("slot_x", [2, NT])
    row_i = sb("row_i", [PAIRS], i32)
    row_f = sb("row_f", [PAIRS + 1])
    rowx_i = sb("rowx_i", [1], i32)
    xtra_i = sb("xtra_i", [2 + 16], i32)
    xtra_f = sb("xtra_f", [2 + 16])

    bank = nc.alloc_psum_tensor("bank", [P, 8, 512], fp32)

    def ps(b, n=512, off=0, lo=0, hi=P):
        return bank[lo:hi, b, off:off + n]

    def ps2(b, n):
        return bank[:, b:b + 2, :].rearrange("p a b -> p (a b)")[:, 0:n]

    class Signal:

        def __init__(self, name, per_layer, credit=0):
            self.sem, self.per_layer, self.credit = nc.alloc_semaphore(name), per_layer, credit

        def at(self, L, k):
            return L * self.per_layer + (self.credit + k)

    STEPS_DVE, STEPS_POOL, STEPS_ACT = 150, 19, 48
    NORMS = 3 * NT
    const_ready = Signal("const_ready", 0)
    loaded = Signal("loaded", 0)
    gains_in = Signal("gains_in", 0)
    r_in = Signal("r_in", 2 * 16)
    rope_ready = Signal("rope_ready", 0)
    h_moe = Signal("h_moe", NT)
    squared = Signal("squared", NORMS)
    rooted = Signal("rooted", NORMS)
    xn_ready = Signal("xn_ready", NORMS)
    flipped = Signal("flipped", NORMS)
    xT_ready = Signal("xT_ready", 2 * NORMS)
    hi_ready, lo_ready, in_done = Signal("hi_ready", IN_UNITS), Signal("lo_ready", IN_UNITS), Signal("in_done", IN_UNITS)
    x_hi_ready, x_lo_ready = Signal("x_hi_ready", NT), Signal("x_lo_ready", NT)
    qk_act, qk_dve = Signal("qk_act", NPAIR), Signal("qk_dve", NPAIR)
    v_out, lat_out = Signal("v_out", NT), Signal("lat_out", 2 * NT)
    lat_sq, lat_root, lat_ready = Signal("lat_sq", NT), Signal("lat_root", NT), Signal("lat_ready", NT)
    lat_flip = Signal("lat_flip", 1)
    cqT_ready, ckvT_ready = Signal("cqT_ready", 1), Signal("ckvT_ready", 1)
    UNITS = NPAIR * NT

    def keys(u):
        return (u % NT + 1) * P

    sb_z, sb_sig, sb_w = Signal("sb_z", UNITS), Signal("sb_sig", 2 * UNITS), Signal("sb_w", 2 * UNITS)
    sb_scan = Signal("sb_scan", 2 * UNITS)
    sb_flip = Signal("sb_flip", UNITS)
    sb_wT = [Signal("sb_wT0", UNITS), Signal("sb_wT1", UNITS)]
    sb_o = Signal("sb_o", UNITS)
    up_done, q_out, k_out = Signal("up_done", 2 * NT), Signal("q_out", NT), Signal("k_out", NT)
    q_rope, k_rope = Signal("q_rope", NT), Signal("k_rope", NT)
    up_flip, qT_out, kT_out = Signal("up_flip", 2 * NT), Signal("qT_out", 2 * NT), Signal("kT_out", 2 * NT)
    ml_z, ml_peak, ml_exp = Signal("ml_z", UNITS), Signal("ml_peak", 2 * UNITS), Signal("ml_exp", 2 * UNITS)
    ml_w, ml_flip = Signal("ml_w", 2 * UNITS), Signal("ml_flip", UNITS)
    ml_wT = [Signal("ml_wT0", UNITS), Signal("ml_wT1", UNITS)]
    ml_o = Signal("ml_o", UNITS)
    o_sq, o_sum = Signal("o_sq", 2 * NPAIR), Signal("o_sum", 2 * NPAIR)
    o_ms, o_ms_out, o_root = Signal("o_ms", 2), Signal("o_ms_out", 2), Signal("o_root", 2)
    wo_done, wo_out = Signal("wo_done", 2 * NT), Signal("wo_out", 2 * NT)
    part_hi, part_lo = Signal("part_hi", NT), Signal("part_lo", NT)
    slot_step = Signal("slot_step", 3 * PAIRS)
    selected = Signal("selected", PAIRS)
    emb_done, emb_out = Signal("emb_done", 2 * NT), Signal("emb_out", 2 * NT)
    r_done, r_out = Signal("r_done", NT), Signal("r_out", 1)
    g_exp, e_in, e_exp = Signal("g_exp", 1), Signal("e_in", 2), Signal("e_exp", 1)
    memb_ready, rank_done = Signal("memb_ready", 1), Signal("rank_done", 1)
    sel_ready, tok_done, tok_ready = Signal("sel_ready", 1), Signal("tok_done", 1), Signal("tok_ready", 1)
    slots_ready = Signal("slots_ready", 1)
    w_qk_in, w_vl_in = [Signal("w_q_in", 16), Signal("w_k_in", 16)], Signal("w_vl_in", 16)
    w_up_in, w_o_in = Signal("w_up_in", 2 * 16), Signal("w_o_in", 16)
    gu_in = [Signal(f"gu_in{b}", 2 * 16 * PAIRS // 2) for b in range(2)]
    dn_in = [Signal(f"dn_in{b}", 16 * PAIRS // 2) for b in range(2)]
    g_flip, xgT_ready = Signal("g_flip", PAIRS), Signal("xgT_ready", 2 * PAIRS)
    gu_done, silu_done, hid_ready = Signal("gu_done", PAIRS), Signal("silu_done", PAIRS), Signal("hid_ready", PAIRS)
    hid_flip, hidT_ready = Signal("hid_flip", PAIRS), Signal("hidT_ready", PAIRS)
    dn_done = Signal("dn_done", PAIRS)
    y_act, y_dve = Signal("y_act", PAIRS, 1), Signal("y_dve", PAIRS, 1)
    y_stored = [Signal(f"y_stored{b}", 16 * PAIRS // 2) for b in range(2)]
    y_free = Signal("y_free", PAIRS, 1)
    x_sel, x_tok, x_row, x_idx, x_w = [nc.alloc_semaphore(n) for n in ("x_sel", "x_tok", "x_row", "x_idx", "x_w")]
    x_flip, x_T, x_gu, x_silu, x_hid = [nc.alloc_semaphore(n) for n in ("x_flip", "x_T", "x_gu", "x_silu", "x_hid")]
    x_hflip, x_hT, x_dn, x_y, x_store = [nc.alloc_semaphore(n) for n in ("x_hflip", "x_hT", "x_dn", "x_y", "x_store")]
    x_over = Signal("x_over", 1)
    back_in = [Signal(f"back_in{t}", 16) for t in range(NT)]
    w_g_in = [Signal("w_g_left", 16), Signal("w_g_right", 16)]
    w_g_last_in, w_e_in = Signal("w_g_last_in", 16), Signal("w_e_in", 2 * 16)
    p_flip, pT_ready = Signal("p_flip", PC), Signal("pT_ready", PC)
    gate_done, gate_out = Signal("gate_done", 2 * NT), Signal("gate_out", 2 * NT)
    ple_out = Signal("ple_out", 2 * NT, 2 * NT)
    act_step, dve_step, pool_step = Signal("act_step", STEPS_ACT), Signal("dve_step", STEPS_DVE), Signal("pool_step", STEPS_POOL)
    fin_eps = nc.alloc_semaphore("fin_eps")
    fin_root, fin_ready = Signal("fin_root", 0), Signal("fin_ready", 0)
    g_last_in, stored = Signal("g_last_in", 0), Signal("stored", 0)

    passed = nc.alloc_semaphore("passed")

    def alone(eng):
        eng.sem_inc(passed, 1)

    class Steps:

        def __init__(self, eng, counted):
            self.eng, self.counted, self.n = eng, counted, 0

        def add(self, L):
            self.n += 1
            return self.counted.sem

        def wait(self, L, back=0):
            self.eng.wait_ge(self.counted.sem, self.counted.at(L, self.n - back))

    def unit_weights(k):
        if k < QK_UNITS:
            return w_qk[:, 4 * (k % 2):4 * (k % 2) + 4, (k // 2) * P:(k // 2 + 1) * P]
        lo, n = GROUPS[(k - QK_UNITS) // DC]
        return w_vl[:, (k - QK_UNITS) % DC, lo:lo + n]

    def unit_part(parts, k):
        if k < QK_UNITS:
            return parts[k % 4].rearrange("p (a b) -> p a b", a=4)
        return parts[k % 4][:, 0:GROUPS[(k - QK_UNITS) // DC][1]]

    with nc.Block() as block:

        @block.sync
        def _(sp):
            x_v = io["x"][0].rearrange("(t p) d -> p t d", p=P)
            sp.dma_start(h, x_v).then_inc(loaded.sem, 16)
            sp.dma_start(pos_i[:], io["positions"][0].rearrange("(t p) -> p t", p=P),
                         allow_slow_non_contiguous=True).then_inc(loaded.sem, 16)
            w_in_v = io["w_in"].rearrange("l (p c) n -> l p c n", c=DC)
            gate_v = io["w_gate"].rearrange("l (n e) (p c) f -> (l n) p e (c f)", e=2, c=DC)
            up_v = io["w_up"].rearrange("l (n e) (p c) f -> (l n) p e (c f)", e=2, c=DC)
            down_v = io["w_down"].rearrange("l (n e) (p c) f -> (l n) p e (c f)", e=2, c=EC)
            for k, name in enumerate(("g_mix", "g_moe", "g_ple")):
                sp.dma_start(g_norm[:, k], io[name].rearrange("l (p c) -> p l c", c=DC)).then_inc(gains_in.sem, 16)
            for to, name in ((g_lat[:, :, 0:QC], "g_cq"), (g_lat[:, :, QC:QC + KVC], "g_ckv"),
                             (g_o[:, :, 0:NPAIR], "g_osb"), (g_o[:, :, NPAIR:2 * NPAIR], "g_omla")):
                for l in range(DEPTH):
                    sp.dma_start(to[:, l], io[name][l].rearrange("(c p) -> p c", p=P),
                                 allow_slow_non_contiguous=True).then_inc(gains_in.sem, 16)
            for l in range(DEPTH):
                sp.dma_start(b_r[:, l, 0:NG], io["b_rg"][l].unsqueeze(0).to_broadcast([P, NG])).then_inc(gains_in.sem, 16)
                sp.dma_start(b_r[:, l, NG:NR], io["b_re"][l].unsqueeze(0).to_broadcast([P, NE])).then_inc(gains_in.sem, 16)
            with sp.Fori(0, DEPTH) as L:
                for k in range(2):
                    cols = slice(k * SBW, (k + 1) * SBW)
                    sp.dma_start(w_qk[:, :, cols], w_in_v[L][:, :, cols]).then_inc(w_qk_in[k].sem, 16)
                sp.dma_start(w_vl, w_in_v[L][:, :, 2 * SBW:IN]).then_inc(w_vl_in.sem, 16)
                sp.dma_start(w_r[:, :, 0:NG], io["w_rg"].rearrange("l (p c) n -> l p c n", c=DC)[L]).then_inc(r_in.sem, 16)
                sp.dma_start(w_r[:, :, NG:NR], io["w_re"].rearrange("l (p c) n -> l p c n", c=DC)[L]).then_inc(r_in.sem, 16)
                sp.wait_ge(in_done.sem, in_done.at(L, IN_UNITS))
                sp.wait_ge(lat_ready.sem, lat_ready.at(L, NT))
                sp.dma_start(w_uq, io["w_uq"].rearrange("l (c p) n -> l p c n", p=P)[L]).then_inc(w_up_in.sem, 16)
                sp.dma_start(w_ukv, io["w_ukv"].rearrange("l (c p) n -> l p c n", p=P)[L]).then_inc(w_up_in.sem, 16)
                sp.dma_start(w_o, io["w_out"].rearrange("l (c p) n -> l p c n", p=P)[L]).then_inc(w_o_in.sem, 16)

                def load_gate_up(n, b):
                    two = w_pair[b]
                    sp.dma_start(two[:, :, 0:DC * DE], gate_v[L * PAIRS + n]).then_inc(gu_in[b].sem, 16)
                    sp.dma_start(two[:, :, DC * DE:2 * DC * DE], up_v[L * PAIRS + n]).then_inc(gu_in[b].sem, 16)

                def load_down(n, b):
                    sp.dma_start(w_pair[b][:, :, 2 * DC * DE:EXPERT], down_v[L * PAIRS + n]).then_inc(dn_in[b].sem, 16)

                load_gate_up(0, 0)
                load_down(0, 0)
                sp.wait_ge(wo_done.sem, wo_done.at(L, 2 * NT))
                load_gate_up(1, 1)
                load_down(1, 1)
                with sp.Fori(0, PAIRS // 2 - 1) as i:
                    for b in range(2):
                        sp.wait_ge(gu_done.sem, gu_done.at(L, 2 * i + b + 1))
                        load_gate_up(2 * i + (b + 2), b)
                        sp.wait_ge(dn_done.sem, dn_done.at(L, 2 * i + b + 1))
                        load_down(2 * i + (b + 2), b)
                sp.wait_ge(dn_done.sem, dn_done.at(L, PAIRS - 1))
                sp.dma_start(w_e, io["w_pe"].rearrange("l (p c) n -> l p c n", c=PC)[L]).then_inc(w_e_in.sem, 16)
                sp.dma_start(p_tok, io["p"].rearrange("l b (t p) n -> (l b) p t n", p=P)[L]).then_inc(w_e_in.sem, 16)
                pg_v = io["w_pg"].rearrange("l (p c) n -> l p c n", c=DC)
                sp.dma_start(w_g[:, :, 0:HALF], pg_v[L][:, 0:DC - 1, 0:HALF]).then_inc(w_g_in[0].sem, 16)
                sp.wait_ge(slots_ready.sem, slots_ready.at(L, 1))
                alone(sp)
                so_far = sp.value_load(xtra_i[0:1, 0:1], min_val=0, max_val=DEPTH * XTRA)
                n_xtra = sp.value_load(xtra_i[0:1, 1:2], min_val=0, max_val=XTRA)
                e_v = [io[n].rearrange("l e (p c) f -> (l e) p (c f)", p=P) for n in ("w_gate", "w_up", "w_down")]
                with sp.If(n_xtra > 0):
                    with sp.Fori(0, XTRA) as j:
                        with sp.If(j < n_xtra):
                            sp.wait_ge(x_idx, so_far + j + 1)
                            alone(sp)
                            e = sp.value_load(xtra_i[0:1, bass.ds(j + 2, 1)], min_val=0, max_val=NE - 1)
                            one = w_pair[1][:, 0]
                            sp.dma_start(one[:, 0:DC * DE], e_v[0][L * NE + e]).then_inc(x_w, 16)
                            sp.dma_start(one[:, DC * DE:2 * DC * DE], e_v[1][L * NE + e]).then_inc(x_w, 16)
                            sp.dma_start(one[:, 2 * DC * DE:EXPERT], e_v[2][L * NE + e]).then_inc(x_w, 16)
                        sp.nop()
                sp.nop()
                sp.wait_ge(dn_done.sem, dn_done.at(L, PAIRS))
                sp.wait_ge(x_over.sem, x_over.at(L, 1))
                for t in range(NT):
                    if t == 1:
                        sp.dma_start(w_g_last, pg_v[L][:, DC - 1]).then_inc(w_g_last_in.sem, 16)
                    if t == 2:
                        sp.dma_start(w_g[:, :, HALF:D], pg_v[L][:, 0:DC - 1, HALF:D]).then_inc(w_g_in[1].sem, 16)
                    if t == NT - 1:
                        sp.wait_ge(h_moe.sem, h_moe.at(L, 1))
                    sp.dma_start(back[t % 3], y_rows.rearrange("(a t p) d -> t p a d", a=2, p=P)[t]).then_inc(back_in[t].sem, 16)
                sp.wait_ge(emb_done.sem, emb_done.at(L, 2 * NT))
                alone(sp)
            sp.wait_ge(gate_done.sem, gate_done.at(DEPTH, 0))
            sp.dma_start(g_last, io["g_final"].unsqueeze(0).to_broadcast([P, D])).then_inc(g_last_in.sem, 16)
            for t in range(NT):
                sp.wait_ge(fin_ready.sem, t + 1)
                sp.dma_start(out[0].rearrange("(t p) d -> t p d", p=P)[t], h[:, t]).then_inc(stored.sem, 16)
            sp.wait_ge(stored.sem, 16 * NT)

        @block.gpsimd
        def _(pool):
            step = Steps(pool, pool_step)
            made = nc.alloc_semaphore("made")
            pool.memset(ident[:], 0.0).then_inc(made, 1)
            pool.memset(sb_mask[:], 0.0).then_inc(made, 1)
            pool.memset(mla_mask[:], 0.0).then_inc(made, 1)
            pool.memset(before_b[:], 1.0).then_inc(made, 1)
            pool.wait_ge(made, 4)
            pool.affine_select(out=ident[:], in_=ident[:], compare_op=ALU.not_equal, fill=1.0, base=0,
                               pattern=[[-1, P]], channel_multiplier=1).then_inc(made, 1)
            pool.affine_select(out=sb_mask[:], in_=sb_mask[:], compare_op=ALU.is_gt, fill=-BIG, base=0,
                               pattern=[[-1, P]], channel_multiplier=1).then_inc(made, 1)
            pool.memset(mla_mask[0:CHUNK, CHUNK:P], -BIG).then_inc(made, 1)
            pool.affine_select(out=before_b[:], in_=before_b[:], compare_op=ALU.is_gt, fill=0.0, base=0,
                               pattern=[[1, P]], channel_multiplier=-1).then_inc(made, 1)
            pool.wait_ge(made, 8)
            pool.tensor_copy(ident_b[:], ident[:]).then_inc(made, 1)
            pool.memset(ones[:], 1.0).then_inc(made, 1)
            pool.memset(ones_b[:], 1.0).then_inc(made, 1)
            pool.memset(minus_half[:], -0.5).then_inc(made, 1)
            pool.memset(xtra_i[:], 0).then_inc(made, 1)
            pool.memset(xtra_f[:], 0.0).then_inc(made, 1)
            pool.iota(expert_no[:], [[1, NE]], base=0, channel_multiplier=0,
                      allow_small_or_imprecise_dtypes=True).then_inc(made, 1)
            pool.iota(pair_slot[:], [[1, P]], base=0, channel_multiplier=0,
                      allow_small_or_imprecise_dtypes=True).then_inc(made, 1)
            pool.iota(row_no[:], [[S, 2], [P, NT]], base=1, channel_multiplier=1,
                      allow_small_or_imprecise_dtypes=True).then_inc(made, 1)
            pool.iota(thresh[:], [[SLOT, 7]], base=SLOT, channel_multiplier=0,
                      allow_small_or_imprecise_dtypes=True).then_inc(made, 1)
            pool.iota(xtra_no[:], [[1, 16]], base=0, channel_multiplier=0,
                      allow_small_or_imprecise_dtypes=True).then_inc(made, 1)
            for k in range(ROPE // 2):
                freq = np.float32(10000.0) ** (-np.float32(2 * k) / np.float32(ROPE))
                pool.memset(inv_freq[:, k:k + 1], float(freq)).then_inc(made, 1)
            pool.wait_ge(made, 19 + ROPE // 2)
            pool.sem_inc(const_ready.sem, 1)

            def root(to, of, before, value, done):
                pool.wait_ge(before.sem, value)
                n = of.shape[1]
                alone(pool)
                pool.tensor_scalar(of, of, EPS, None, ALU.add).then_inc(step.add(0), 1)
                step.wait(layer[0])
                pool.tensor_tensor(to, of, minus_half[:, 0:n], ALU.pow).then_inc(done.sem, 1)

            layer = [None]
            with pool.Fori(0, DEPTH) as L:
                layer[0] = L
                step.n = 0
                for t in range(NT):
                    root(rstd[:, t:t + 1], ms[:, t:t + 1], squared, squared.at(L, t + 1), rooted)
                for t in range(NT - 1):
                    pool.wait_ge(x_hi_ready.sem, x_hi_ready.at(L, t + 1))
                    pool.tensor_tensor(x_lo[:, :, t * P:(t + 1) * P], x_tile[t % 2], x_hi[:, :, t * P:(t + 1) * P].bitcast(fp32),
                                       ALU.subtract).then_inc(x_lo_ready.sem, 1)
                for t in range(NT):
                    root(rstd_lat[:, t], ms_lat[:, t], lat_sq, lat_sq.at(L, t + 1), lat_root)
                pool.wait_ge(lat_flip.sem, lat_flip.at(L, 1))
                alone(pool)
                pool.memset(stay[:, :, :, S:S + 2].rearrange("p a b c -> p (a b) c"), 1.0).then_inc(step.add(L), 1)
                step.wait(L)

                def add_squares(kind, m):
                    pool.wait_ge(o_sq.sem, o_sq.at(L, kind * NPAIR + m + 1))
                    if m == 0:
                        alone(pool)
                        pool.tensor_copy(o_total[kind], o_square[kind][:, m % 2]).then_inc(o_sum.sem, 1)
                    else:
                        pool.wait_ge(o_sum.sem, o_sum.at(L, kind * NPAIR + m))
                        pool.tensor_tensor(o_total[kind], o_total[kind], o_square[kind][:, m % 2], ALU.add).then_inc(o_sum.sem, 1)

                for u in range(UNITS):
                    n = keys(u)
                    for s in range(2):
                        pool.wait_ge(sb_scan.sem, sb_scan.at(L, 2 * u + s + 1))
                        pool.tensor_tensor(take[:, u % 2, s, S - n:S], take[:, u % 2, s, S - n:S],
                                           stay[:, u % 2, s, S - n + 1:S + 1], ALU.mult).then_inc(sb_w.sem, 1)
                    if u % NT == 1 and u > NT:
                        add_squares(0, u // NT - 1)
                add_squares(0, NPAIR - 1)
                root(rstd_o[:, 0], ms_o[:, 0], o_ms_out, o_ms_out.at(L, 1), o_root)
                for m in range(NPAIR):
                    add_squares(1, m)
                root(rstd_o[:, 1], ms_o[:, 1], o_ms_out, o_ms_out.at(L, 2), o_root)
                for t in range(NT):
                    n = NT + t
                    root(rstd[:, n:n + 1], ms[:, n:n + 1], squared, squared.at(L, n + 1), rooted)
                    pool.wait_ge(part_hi.sem, part_hi.at(L, t + 1))
                    pool.tensor_tensor(x_parts[:, 1, t], xn[t % 2], x_parts[:, 0, t].bitcast(fp32), ALU.subtract).then_inc(part_lo.sem, 1)
                pool.wait_ge(tok_ready.sem, tok_ready.at(L, 1))

                def stored_rows(n):
                    pool.wait_ge(y_stored[n % 2].sem, y_stored[n % 2].at(L, 16 * (n // 2 + 1)))
                    pool.sem_inc(y_free.sem, 1)

                to_row = dict(bounds_check=2 * S - 1, oob_is_err=False)
                for n in range(PAIRS):
                    pool.wait_ge(y_act.sem, y_act.at(L, n + 1))
                    pool.wait_ge(y_dve.sem, y_dve.at(L, n + 1))
                    alone(pool)
                    pool.indirect_dma_start(out=y_rows, out_offset=bass.IndirectOffsetOnAxis(ap=row_i[:, n:n + 1], axis=0),
                                            in_=y_out[n % 2], in_offset=None, **to_row).then_inc(y_stored[n % 2].sem, 16)
                    if n:
                        stored_rows(n - 1)
                stored_rows(PAIRS - 1)
                pool.wait_ge(slots_ready.sem, slots_ready.at(L, 1))
                alone(pool)
                so_far = pool.value_load(xtra_i[0:1, 0:1], min_val=0, max_val=DEPTH * XTRA)
                n_xtra = pool.value_load(xtra_i[0:1, 1:2], min_val=0, max_val=XTRA)
                with pool.If(n_xtra > 0):
                    with pool.Fori(0, XTRA) as j:
                        with pool.If(j < n_xtra):
                            pool.wait_ge(x_y, so_far + j + 1)
                            alone(pool)
                            pool.indirect_dma_start(out=y_rows, out_offset=bass.IndirectOffsetOnAxis(ap=rowx_i[0:SLOT, :], axis=0),
                                                    in_=y_out[0][0:SLOT], in_offset=None, **to_row).then_inc(x_store, 16)
                            pool.wait_ge(x_store, 16 * (so_far + j + 1))
                            alone(pool)
                        pool.nop()
                pool.nop()
                pool.sem_inc(x_over.sem, 1)
                for t in range(2 * NT, 3 * NT):
                    root(rstd[:, t:t + 1], ms[:, t:t + 1], squared, squared.at(L, t + 1), rooted)
            assert step.n == STEPS_POOL, step.n
            for t in range(NT):
                pool.wait_ge(squared.sem, squared.at(DEPTH, t + 1))
                pool.tensor_scalar(ms[:, t:t + 1], ms[:, t:t + 1], EPS, None, ALU.add).then_inc(fin_eps, 1)
                pool.wait_ge(fin_eps, t + 1)
                pool.tensor_tensor(rstd[:, 12 + t:13 + t], ms[:, t:t + 1], minus_half[:, 0:1], ALU.pow).then_inc(fin_root.sem, 1)

        @block.scalar
        def _(act):
            step = Steps(act, act_step)
            act.sem_inc(y_act.sem, 1)
            act.sem_inc(y_free.sem, 2)
            act.wait_ge(loaded.sem, 32)
            for t in range(NT):
                act.activation(junk[:], h[:, t], ACT.Square, scale=D ** -0.5, accum_out=ms[:, t:t + 1]).then_inc(squared.sem, 1)
                act.wait_ge(squared.sem, t + 1)
            act.wait_ge(rope_ready.sem, 2)
            act.activation(sin[:].rearrange("p a b -> p (a b)"), red[:].rearrange("p a b -> p (a b)"), ACT.Sin).then_inc(rope_ready.sem, 1)
            act.activation(cos[:].rearrange("p a b -> p (a b)"), turn[:].rearrange("p a b -> p (a b)"), ACT.Sin).then_inc(rope_ready.sem, 1)

            with act.Fori(0, DEPTH) as L:
                step.n = 0

                def mean_square(stage, t, source, value):
                    n = stage * NT + t
                    act.wait_ge(source.sem, source.at(L, value))
                    act.activation(junk[:], h[:, t], ACT.Square, scale=D ** -0.5,
                                   accum_out=ms[:, n % NORMS:n % NORMS + 1]).then_inc(squared.sem, 1)
                    act.wait_ge(squared.sem, squared.at(L, n + 1))

                for t in range(NT):
                    if t == 2:
                        act.wait_ge(w_qk_in[0].sem, w_qk_in[0].at(L, 16))
                        for k in range(4):
                            act.activation(unit_part(w_hi, k), unit_weights(k), ACT.Copy).then_inc(hi_ready.sem, 1)
                    act.wait_ge(xT_ready.sem, xT_ready.at(L, 2 * (t + 1)))
                    act.activation(x_hi[:, :, t * P:(t + 1) * P], x_tile[t % 2], ACT.Copy).then_inc(x_hi_ready.sem, 1)
                for k in range(4, IN_UNITS):
                    if k == QK_UNITS // 2:
                        act.wait_ge(w_qk_in[1].sem, w_qk_in[1].at(L, 16))
                    if k == QK_UNITS:
                        act.wait_ge(w_vl_in.sem, w_vl_in.at(L, 16))
                    act.wait_ge(in_done.sem, in_done.at(L, k - 3))
                    act.activation(unit_part(w_hi, k), unit_weights(k), ACT.Copy).then_inc(hi_ready.sem, 1)
                    if k % 4 == 1 and 4 < k < 4 + QK_UNITS:
                        m = (k - 5) // 2
                        to = qT_sb[:, m] if m < NPAIR else kT_sb[:, m - NPAIR]
                        act.activation(to, ps(4 + m % 4), ACT.Copy).then_inc(qk_act.sem, 1)
                for t in range(NT):
                    act.wait_ge(lat_out.sem, lat_out.at(L, NT + t + 1))
                    act.activation(junk[:, 0:QR], lat[:, t, 0:QR], ACT.Square, scale=QR ** -0.5,
                                   accum_out=ms_lat[:, t, 0:1]).then_inc(step.add(L), 1)
                    step.wait(L)
                    act.activation(junk[:, 0:KVR], lat[:, t, QR:QR + KVR], ACT.Square, scale=KVR ** -0.5,
                                   accum_out=ms_lat[:, t, 1:2]).then_inc(lat_sq.sem, 1)
                    act.wait_ge(lat_sq.sem, lat_sq.at(L, t + 1))
                act.wait_ge(in_done.sem, in_done.at(L, IN_UNITS))
                for t in range(NT):
                    act.activation(v_att[:, t], ps(t), ACT.Copy).then_inc(v_out.sem, 1)
                act.wait_ge(lat_flip.sem, lat_flip.at(L, 1))
                act.wait_ge(gains_in.sem, 16 * (3 + 6 * DEPTH))
                for j in range(QC):
                    to = act.activation(cqT[:, j], ps(3 + j), ACT.Copy, scale=g_lat[:, L, j:j + 1])
                to.then_inc(cqT_ready.sem, 1)

                def pair_out(kind, m, done):
                    k = kind * NPAIR + m
                    act.wait_ge(done.sem, done.at(L, (m + 1) * NT))
                    act.activation(oT[:, k], ps(6 + m % 2), ACT.Copy, scale=g_o[:, L, k:k + 1]).then_inc(step.add(L), 1)
                    if m >= 2:
                        act.wait_ge(o_sum.sem, o_sum.at(L, k - 1))
                    act.activation(o_square[kind][:, m % 2], ps(6 + m % 2), ACT.Square).then_inc(o_sq.sem, 1)

                for u in range(UNITS + 1):
                    if u < UNITS:
                        n = keys(u)
                        act.wait_ge(sb_z.sem, sb_z.at(L, u + 1))
                        for s in range(2):
                            z = ps(2 * (u % 2) + s, n)
                            act.activation(stay[:, u % 2, s, S - n:S], z, ACT.Sigmoid, scale=-SB_SCALE).then_inc(step.add(L), 1)
                            act.activation(take[:, u % 2, s, S - n:S], z, ACT.Sigmoid, scale=SB_SCALE).then_inc(sb_sig.sem, 1)
                    if u >= 1:
                        v = u - 1
                        n = keys(v)
                        act.wait_ge(sb_flip.sem, sb_flip.at(L, v + 1))
                        act.activation(wT[:, v % 2, 0, 0:n], ps(4, n), ACT.Copy).then_inc(sb_wT[0].sem, 1)
                        if v % NT == 0 and v:
                            pair_out(0, v // NT - 1, sb_o)
                pair_out(0, NPAIR - 1, sb_o)
                for t in range(NT + 1):
                    if t < NT:
                        act.wait_ge(up_done.sem, up_done.at(L, 2 * t + 1))
                        if t:
                            act.wait_ge(up_flip.sem, up_flip.at(L, 2 * t - 1))
                        act.activation(q_tok.rearrange("p a b -> p (a b)"), ps2(0, NH * QK), ACT.Copy,
                                       scale=MLA_SCALE).then_inc(q_out.sem, 1)
                        act.wait_ge(up_done.sem, up_done.at(L, 2 * t + 2))
                        if t:
                            act.wait_ge(up_flip.sem, up_flip.at(L, 2 * t))
                        kv = ps2(2, NH * 2 * HD).rearrange("p (a b) -> p a b", a=NH)
                        act.activation(k_tok[:, :, 0:HD], kv[:, :, 0:HD], ACT.Copy).then_inc(step.add(L), 1)
                        act.activation(v_att[:, t].rearrange("p (a b) -> p a b", a=NH), kv[:, :, HD:2 * HD],
                                       ACT.Copy).then_inc(k_out.sem, 1)
                    if t:
                        v = t - 1
                        act.wait_ge(up_flip.sem, up_flip.at(L, 2 * v + 1))
                        for g in range(2):
                            act.activation(qT[0:QK, 4 * g:4 * g + 4, v * P:(v + 1) * P],
                                           ps(4 + g, hi=QK).rearrange("p (a b) -> p a b", a=4), ACT.Copy).then_inc(qT_out.sem, 1)
                for u in range(UNITS + 1):
                    if u < UNITS:
                        n = keys(u)
                        for s in range(2):
                            act.wait_ge(ml_peak.sem, ml_peak.at(L, 2 * u + s + 1))
                            act.activation(prob[:, u % 2, s, 0:n], ps(2 * (u % 2) + s, n), ACT.Exp,
                                           bias=peak[:, u % 2, s:s + 1], accum_out=rsum[:, u % 2, s:s + 1]).then_inc(ml_exp.sem, 1)
                    if u >= 1:
                        v = u - 1
                        n = keys(v)
                        act.wait_ge(ml_flip.sem, ml_flip.at(L, v + 1))
                        act.activation(pTr[:, v % 2, 0, 0:n], ps(4, n), ACT.Copy).then_inc(ml_wT[0].sem, 1)
                        if v % NT == 0 and v:
                            pair_out(1, v // NT - 1, ml_o)
                pair_out(1, NPAIR - 1, ml_o)
                for t in range(NT):
                    mean_square(1, t, wo_out, 2 * (t + 1))
                    act.wait_ge(xn_ready.sem, xn_ready.at(L, NT + t + 1))
                    act.activation(x_parts[:, 0, t], xn[t % 2], ACT.Copy).then_inc(part_hi.sem, 1)
                act.wait_ge(e_in.sem, e_in.at(L, 1))
                act.activation(gsc[:, :, 0:NG], gsc[:, :, 0:NG], ACT.Exp).then_inc(g_exp.sem, 1)
                act.wait_ge(e_in.sem, e_in.at(L, 2))
                act.activation(top_w[:, 1], top_w[:, 1], ACT.Exp).then_inc(e_exp.sem, 1)

                with act.Fori(0, PAIRS // 2) as i:
                    for b in range(2):
                        n = 2 * i + b
                        act.wait_ge(gu_done.sem, gu_done.at(L, n + 1))
                        act.activation(silu[b], ps(2 + b, DE), ACT.Silu).then_inc(silu_done.sem, 1)
                        act.wait_ge(hid_flip.sem, hid_flip.at(L, n + 1))
                        act.activation(hidT[b], ps(5, EC * P).rearrange("p (a b) -> p a b", a=EC), ACT.Copy).then_inc(hidT_ready.sem, 1)
                        act.wait_ge(dn_done.sem, dn_done.at(L, n + 1))
                        act.wait_ge(y_free.sem, y_free.at(L, n))
                        act.activation(y_out[b][:, HALF:D], ps(7), ACT.Copy).then_inc(y_act.sem, 1)
                act.wait_ge(p_flip.sem, p_flip.at(L, PC))
                for j in range(PC):
                    act.activation(pT[:, j], ps(4 + j), ACT.Copy).then_inc(pT_ready.sem, 1)
                act.wait_ge(slots_ready.sem, slots_ready.at(L, 1))
                alone(act)
                so_far = act.value_load(xtra_i[0:1, 0:1], min_val=0, max_val=DEPTH * XTRA)
                n_xtra = act.value_load(xtra_i[0:1, 1:2], min_val=0, max_val=XTRA)
                with act.If(n_xtra > 0):
                    with act.Fori(0, XTRA) as j:
                        with act.If(j < n_xtra):
                            act.wait_ge(x_gu, so_far + j + 1)
                            act.activation(silu[0][0:SLOT], ps(2, DE, hi=SLOT), ACT.Silu).then_inc(x_silu, 1)
                        act.nop()
                act.nop()
                for k in range(2 * NT):
                    if k == NT:
                        act.wait_ge(x_over.sem, x_over.at(L, 1))
                    act.wait_ge(emb_done.sem, emb_done.at(L, k + 1))
                    act.activation(emb[:, k // 2, (k % 2) * HALF:(k % 2 + 1) * HALF], ps(4 + k % 2), ACT.Copy).then_inc(emb_out.sem, 1)
                    if k == 3 or k == 6:
                        mean_square(2, k // 3 - 1, h_moe, k // 3)
                for t in range(2, NT):
                    mean_square(2, t, h_moe, t + 1)
                for k in range(2 * NT):
                    act.wait_ge(gate_done.sem, gate_done.at(L, k + 1))
                    if k >= 2:
                        act.wait_ge(ple_out.sem, ple_out.at(L, k - 1))
                    act.activation(gate_s[k % 2], ps(6 + k % 2), ACT.Sigmoid).then_inc(gate_out.sem, 1)
                    if k % 2 == 1 and k >= 3:
                        mean_square(3, k // 2 - 1, ple_out, k - 1)
                mean_square(3, NT - 1, ple_out, 2 * NT)
            assert step.n == STEPS_ACT, step.n
        @block.vector
        def _(dve):
            step = Steps(dve, dve_step)
            rstep = nc.alloc_semaphore("rstep")
            rn = [0]

            def link(ins):
                rn[0] += 1
                ins.then_inc(rstep, 1)
                dve.wait_ge(rstep, rn[0])

            dve.sem_inc(y_dve.sem, 1)
            dve.wait_ge(loaded.sem, 32)
            dve.wait_ge(const_ready.sem, 1)
            NF = ROPE // 2
            link(dve.tensor_copy(pos_f[:], pos_i[:]))
            link(dve.tensor_tensor(ang, pos_f[:].unsqueeze(2).to_broadcast([P, NT, NF]),
                                   inv_freq[:].unsqueeze(1).to_broadcast([P, NT, NF]), ALU.mult))
            two_pi = 2 * np.pi
            parts, left = [], two_pi
            for bits in (5, 9, 9):
                scale = 2.0 ** (bits - 1 - np.floor(np.log2(abs(left))))
                parts.append(float(np.round(left * scale) / scale))
                left -= parts[-1]
            parts.append(float(np.float32(left)))
            for whole, arg, quarter in ((turn, red, 0.0), (cos, turn, 0.25)):
                link(dve.tensor_scalar(whole[:], ang, float(1 / two_pi), quarter, ALU.mult, ALU.add))
                link(dve.tensor_scalar(whole[:], whole[:], ROUND, None, ALU.add))
                link(dve.tensor_scalar(whole[:], whole[:], ROUND, None, ALU.subtract))
                source = ang
                for c in parts:
                    link(dve.scalar_tensor_tensor(arg[:], whole[:], -c, source[:], ALU.mult, ALU.add))
                    source = arg
                if quarter:
                    link(dve.tensor_scalar(arg[:], arg[:], float(np.pi / 2), None, ALU.add))
                dve.tensor_scalar(arg[:], arg[:], 3.1415925, -3.1415925, ALU.min, ALU.max).then_inc(rope_ready.sem, 1)
                dve.wait_ge(rope_ready.sem, 1 if not quarter else 2)
            dve.wait_ge(rope_ready.sem, 4)
            dve.sem_inc(ple_out.sem, 2 * NT)

            with dve.Fori(0, DEPTH) as L:
                step.n = 0

                def norm(stage):
                    for t in range(NT + 1):
                        if t < NT:
                            scaled(stage, t)
                        if t:
                            turned(stage, t - 1, 2 * ((t - 1) % 2))

                def low_weights(k):
                    dve.wait_ge(hi_ready.sem, hi_ready.at(L, k + 1))
                    dve.tensor_tensor(unit_part(w_lo, k), unit_weights(k), unit_part(w_hi, k).bitcast(fp32),
                                      ALU.subtract).then_inc(lo_ready.sem, 1)

                def scaled(stage, t):
                    n = stage * NT + t
                    dve.wait_ge(rooted.sem, rooted.at(L, n + 1))
                    dve.tensor_scalar(xn[t % 2].rearrange("p (c q) -> p q c", c=DC),
                                      h[:, t].rearrange("p (q c) -> p q c", c=DC),
                                      rstd[:, n:n + 1], None, ALU.mult).then_inc(xn_ready.sem, 1)

                def turned(stage, t, b):
                    dve.wait_ge(flipped.sem, flipped.at(L, stage * NT + t + 1))
                    if stage == 0 and t >= 2:
                        dve.wait_ge(x_lo_ready.sem, x_lo_ready.at(L, t - 1))
                    for g in range(2):
                        gain = g_norm[:, stage, L, 4 * g:4 * g + 4]
                        to = x_tile[t % 2][:, 4 * g:4 * g + 4] if stage == 0 else xT[:, 4 * g:4 * g + 4, t * P:(t + 1) * P]
                        dve.tensor_tensor(to,
                                          ps(b + g).rearrange("p (a b) -> p a b", a=4),
                                          gain.unsqueeze(2).to_broadcast([P, 4, P]), ALU.mult).then_inc(xT_ready.sem, 1)

                def rope(x1, x2, t, heads, to1, to2, done, temp):
                    c = cos[:, t].unsqueeze(1).to_broadcast([P, heads, NF])
                    s = sin[:, t].unsqueeze(1).to_broadcast([P, heads, NF])
                    for k, (x, f) in enumerate(((x1, c), (x2, s), (x2, c), (x1, s))):
                        dve.tensor_tensor(temp[:, k], x, f, ALU.mult).then_inc(step.add(L), 1)
                    step.wait(L)
                    dve.tensor_tensor(to1, temp[:, 0], temp[:, 1], ALU.subtract).then_inc(step.add(L), 1)
                    dve.tensor_tensor(to2, temp[:, 2], temp[:, 3], ALU.add).then_inc(done.sem, 1)

                dve.wait_ge(gains_in.sem, 16 * (3 + 6 * DEPTH))
                norm(0)
                for k in range(2):
                    low_weights(k)
                dve.wait_ge(x_hi_ready.sem, x_hi_ready.at(L, NT))
                dve.tensor_tensor(x_lo[:, :, S - P:S], x_tile[(NT - 1) % 2], x_hi[:, :, S - P:S].bitcast(fp32),
                                  ALU.subtract).then_inc(x_lo_ready.sem, 1)
                for k in range(2, IN_UNITS):
                    low_weights(k)
                    if k % 4 == 3 and 4 < k < 4 + QK_UNITS:
                        m = (k - 5) // 2
                        to = qT_sb[:, m] if m < NPAIR else kT_sb[:, m - NPAIR]
                        dve.tensor_copy(to, ps(4 + m % 4)).then_inc(qk_dve.sem, 1)
                    for g in range(2):
                        if k == QK_UNITS + (g + 1) * DC + 3:
                            for t in range(NT):
                                dve.tensor_copy(lat[:, t, g * LAT // 2:(g + 1) * LAT // 2], ps(4 * g + t, LAT // 2)).then_inc(lat_out.sem, 1)
                for v in range(NT):
                    dve.wait_ge(lat_root.sem, lat_root.at(L, v + 1))
                    dve.tensor_scalar(lat[:, v, 0:QR], lat[:, v, 0:QR], rstd_lat[:, v, 0:1], None, ALU.mult).then_inc(step.add(L), 1)
                    dve.tensor_scalar(lat[:, v, QR:QR + KVR], lat[:, v, QR:QR + KVR], rstd_lat[:, v, 1:2], None,
                                      ALU.mult).then_inc(step.add(L), 1)
                    dve.wait_ge(lat_out.sem, lat_out.at(L, 2 * NT))
                    if v:
                        dve.wait_ge(lat_ready.sem, lat_ready.at(L, v))
                    at = QR + KVR
                    rope(lat[:, v, at:at + NF].unsqueeze(1), lat[:, v, at + NF:at + ROPE].unsqueeze(1), v, 1,
                         k_rot[:, v:v + 1, 0:NF], k_rot[:, v:v + 1, NF:ROPE], lat_ready, rope_k)
                dve.wait_ge(lat_flip.sem, lat_flip.at(L, 1))
                for j in range(KVC):
                    to = dve.tensor_scalar(ckvT[:, j], ps(6 + j), g_lat[:, L, QC + j:QC + j + 1], None, ALU.mult)
                to.then_inc(ckvT_ready.sem, 1)
                for u in range(UNITS + 1):
                    if u < UNITS:
                        n = keys(u)
                        for s in range(2):
                            dve.wait_ge(sb_sig.sem, sb_sig.at(L, 2 * u + s + 1))
                            run = stay[:, u % 2, s, S - n:S][:, ::-1]
                            dve.tensor_tensor_scan(run, run, ones[:, 0:1].to_broadcast([P, n]), 1.0, ALU.mult,
                                                   ALU.mult).then_inc(sb_scan.sem, 1)
                    if u:
                        v = u - 1
                        n = keys(v)
                        dve.wait_ge(sb_flip.sem, sb_flip.at(L, v + 1))
                        dve.tensor_copy(wT[:, v % 2, 1, 0:n], ps(5, n)).then_inc(sb_wT[1].sem, 1)
                for t in range(NT + 1):
                    if t < NT:
                        if t == 1:
                            dve.wait_ge(o_ms.sem, o_ms.at(L, 1))
                            dve.tensor_scalar(ms_o[:, 0], ps(7, NT), 1.0 / SBW, None, ALU.mult).then_inc(o_ms_out.sem, 1)
                        dve.wait_ge(q_out.sem, q_out.at(L, t + 1))
                        if t:
                            dve.wait_ge(q_rope.sem, q_rope.at(L, t))
                        else:
                            dve.wait_ge(lat_ready.sem, lat_ready.at(L, NT))
                        rope(q_tok[:, :, HD:HD + NF], q_tok[:, :, HD + NF:QK], t, NH,
                             q_tok[:, :, HD:HD + NF], q_tok[:, :, HD + NF:QK], q_rope, rope_t)
                        dve.wait_ge(k_out.sem, k_out.at(L, t + 1))
                        dve.tensor_copy(k_tok[:, :, HD:QK], k_rot[:, t].unsqueeze(1).to_broadcast([P, NH, ROPE])
                                        ).then_inc(k_rope.sem, 1)
                    if t:
                        v = t - 1
                        dve.wait_ge(up_flip.sem, up_flip.at(L, 2 * v + 2))
                        for g in range(2):
                            dve.tensor_copy(kT[0:QK, 4 * g:4 * g + 4, v * P:(v + 1) * P],
                                            ps(6 + g, hi=QK).rearrange("p (a b) -> p a b", a=4)).then_inc(kT_out.sem, 1)
                def divide(v):
                    n = keys(v)
                    dve.wait_ge(ml_exp.sem, ml_exp.at(L, 2 * v + 2))
                    dve.reciprocal(rinv[:, v % 2], rsum[:, v % 2]).then_inc(step.add(L), 1)
                    step.wait(L)
                    for s in range(2):
                        dve.tensor_scalar(prob[:, v % 2, s, 0:n], prob[:, v % 2, s, 0:n], rinv[:, v % 2, s:s + 1], None,
                                          ALU.mult).then_inc(ml_w.sem, 1)

                for u in range(UNITS + 1):
                    if u < UNITS:
                        dve.wait_ge(ml_z.sem, ml_z.at(L, u + 1))
                        for s in range(2):
                            dve.tensor_reduce(peak[:, u % 2, s:s + 1], ps(2 * (u % 2) + s, keys(u)), axis=AX.X, op=ALU.max,
                                              negate=True).then_inc(ml_peak.sem, 1)
                    if u == 1:
                        divide(0)
                    if u:
                        v = u - 1
                        dve.wait_ge(ml_flip.sem, ml_flip.at(L, v + 1))
                        dve.tensor_copy(pTr[:, v % 2, 1, 0:keys(v)], ps(5, keys(v))).then_inc(ml_wT[1].sem, 1)
                        if u < UNITS:
                            divide(u)
                for k in range(2 * NT):
                    t, half = k // 2, k % 2
                    part = h[:, t, half * HALF:(half + 1) * HALF]
                    b = 2 * (k % 2)
                    if k == 0:
                        dve.wait_ge(o_ms.sem, o_ms.at(L, 2))
                        dve.tensor_scalar(ms_o[:, 1], ps(5, NT), 1.0 / SBW, None, ALU.mult).then_inc(o_ms_out.sem, 1)
                        dve.wait_ge(o_root.sem, o_root.at(L, 2))
                    dve.wait_ge(wo_done.sem, wo_done.at(L, k + 1))
                    dve.scalar_tensor_tensor(part, ps(b), rstd_o[:, 0, t:t + 1], part, ALU.mult, ALU.add).then_inc(step.add(L), 1)
                    step.wait(L)
                    dve.scalar_tensor_tensor(part, ps(b + 1), rstd_o[:, 1, t:t + 1], part, ALU.mult, ALU.add).then_inc(wo_out.sem, 1)
                    if half == 0 and t:
                        turned(1, t - 1, 6)
                    if half == 1:
                        if t >= 2:
                            dve.wait_ge(part_lo.sem, part_lo.at(L, t - 1))
                        scaled(1, t)
                turned(1, NT - 1, 6)

                def do(ins):
                    ins.then_inc(step.add(L), 1)
                    step.wait(L)

                four = [P, NT, NE]
                e_bc = expert_no[:].unsqueeze(1).to_broadcast(four)
                dve.wait_ge(r_done.sem, r_done.at(L, NT))
                dve.tensor_tensor(logit, ps(4, NT * NR).rearrange("p (a b) -> p a b", a=NT),
                                  b_r[:, L].unsqueeze(1).to_broadcast([P, NT, NR]), ALU.add).then_inc(r_out.sem, 1)
                do(dve.memset(g8, -BIG))
                dve.wait_ge(r_out.sem, r_out.at(L, 1))
                do(dve.tensor_copy(g8[:, :, 0:NG], logit[:, :, 0:NG]))
                for t in range(NT):
                    alone(dve)
                    dve.max(best8[:, t], g8[:, t]).then_inc(step.add(L), 1)
                step.wait(L)
                for t in range(NT):
                    alone(dve)
                    dve.max_index(g_i[:, t], best8[:, t], g8[:, t]).then_inc(step.add(L), 1)
                dve.tensor_tensor(gsc[:, :, 0:NG], logit[:, :, 0:NG], best8[:, :, 0:1].to_broadcast([P, NT, NG]),
                                  ALU.subtract).then_inc(e_in.sem, 1)
                step.wait(L)
                do(dve.tensor_copy(g_f[:], g_i[:, :, 0]))
                do(dve.tensor_tensor(gsc[:, :, NG:2 * NG], expert_no[:, 0:NG].unsqueeze(1).to_broadcast([P, NT, NG]),
                                     g_f[:].unsqueeze(2).to_broadcast([P, NT, NG]), ALU.is_equal))
                group = gsc[:, :, NG:2 * NG].unsqueeze(3).to_broadcast([P, NT, NG, EG])
                by_group = rtmp.rearrange("p t (g e) -> p t g e", g=NG)
                do(dve.tensor_tensor(by_group, logit[:, :, NG:NR].rearrange("p t (g e) -> p t g e", g=NG), group, ALU.mult))
                do(dve.tensor_scalar(gsc[:, :, NG:2 * NG], gsc[:, :, NG:2 * NG], BIG, -BIG, ALU.mult, ALU.add))
                do(dve.tensor_tensor(by_group, by_group, group, ALU.add))
                dve.wait_ge(e_in.sem, e_in.at(L, 1))
                for t in range(NT):
                    alone(dve)
                    dve.max(best8[:, t], rtmp[:, t]).then_inc(step.add(L), 1)
                step.wait(L)
                for t in range(NT):
                    alone(dve)
                    dve.max_index(best_i[:, t], best8[:, t], rtmp[:, t]).then_inc(step.add(L), 1)
                step.wait(L)
                do(dve.tensor_copy(best_f[:], best_i[:, :, 0:2]))
                for a in range(2):
                    dve.tensor_tensor(chosen[:, a], e_bc, best_f[:, :, a:a + 1].to_broadcast(four), ALU.is_equal).then_inc(step.add(L), 1)
                step.wait(L)
                dve.tensor_tensor(memb_b[:], chosen[:, 0], chosen[:, 1], ALU.add).then_inc(memb_ready.sem, 1)
                dve.tensor_tensor(top_w[:, 1], best8[:, :, 1], best8[:, :, 0], ALU.subtract).then_inc(e_in.sem, 1)
                dve.wait_ge(g_exp.sem, g_exp.at(L, 1))
                do(dve.tensor_reduce(gp[:], gsc[:, :, 0:NG], axis=AX.X, op=ALU.add))
                do(dve.reciprocal(gp[:], gp[:]))
                dve.wait_ge(e_exp.sem, e_exp.at(L, 1))
                do(dve.tensor_scalar(top_w[:, 0], top_w[:, 1], 1.0, None, ALU.add))
                do(dve.reciprocal(top_w[:, 0], top_w[:, 0]))
                do(dve.tensor_tensor(top_w[:, 0], top_w[:, 0], gp[:], ALU.mult))
                do(dve.tensor_tensor(top_w[:, 1], top_w[:, 1], top_w[:, 0], ALU.mult))
                dve.wait_ge(rank_done.sem, rank_done.at(L, 1))
                do(dve.tensor_copy(rank, ps(5, NT * NE).rearrange("p (a b) -> p a b", a=NT)))
                for a in range(2):
                    do(dve.tensor_tensor(over, chosen[:, a], rank, ALU.mult))
                    do(dve.tensor_reduce(rank_f[:, a], over, axis=AX.X, op=ALU.add))
                do(dve.tensor_scalar(slot_x[:], rank_f[:], float(SLOT), float(2 * MAIN), ALU.is_ge, ALU.mult))
                do(dve.tensor_tensor(slot_x[:], slot_x[:], rank_f[:], ALU.add))
                do(dve.scalar_tensor_tensor(slot_x[:], best_f[:].rearrange("p t a -> p a t"), float(SLOT), slot_x[:], ALU.mult, ALU.add))
                by_slot = pair_slot[:].unsqueeze(1).to_broadcast([P, NT, P])

                def slots_of(of, a):
                    return of[:, a].unsqueeze(2).to_broadcast([P, NT, P])

                def select(n, half):
                    dve.tensor_tensor(sel_half, by_slot, slots_of(slot_x, 0), ALU.is_equal).then_inc(slot_step.sem, 1)
                    dve.tensor_tensor(sel_other, by_slot, slots_of(slot_x, 1), ALU.is_equal).then_inc(slot_step.sem, 1)
                    dve.wait_ge(slot_step.sem, slot_step.at(L, 3 * n + 2))
                    dve.tensor_scalar(slot_x[:], slot_x[:], float(-P), None, ALU.add).then_inc(slot_step.sem, 1)
                    dve.tensor_tensor(sel[:, :, half * P:(half + 1) * P], sel_other, sel_half, ALU.add).then_inc(selected.sem, 1)
                    dve.wait_ge(slot_step.sem, slot_step.at(L, 3 * n + 3))
                    dve.wait_ge(selected.sem, selected.at(L, n + 1))

                select(0, 0)
                select(1, 1)
                for a in range(2):
                    dve.tensor_tensor(sel_tok[:, a * NT:(a + 1) * NT], chosen[:, a], row_no[:, a].unsqueeze(2).to_broadcast(four),
                                      ALU.mult).then_inc(step.add(L), 1)
                step.wait(L)
                dve.tensor_tensor(sel_rank.rearrange("p k (e s) -> p k e s", e=2),
                                  pair_slot[:, 0:SLOT].unsqueeze(1).unsqueeze(1).to_broadcast([P, 2 * NT, 2, SLOT]),
                                  rank_f[:].rearrange("p a t -> p (a t)").unsqueeze(2).unsqueeze(3).to_broadcast([P, 2 * NT, 2, SLOT]),
                                  ALU.is_equal).then_inc(sel_ready.sem, 1)
                dve.wait_ge(tok_done.sem, tok_done.at(L, 1))
                dve.tensor_copy(row_f[0:SLOT, 0:PAIRS], ps(6, NE, hi=SLOT)[:, 0:NE:2]).then_inc(step.add(L), 1)
                do(dve.tensor_copy(row_f[SLOT:P, 0:PAIRS], ps(6, NE, lo=SLOT)[:, 1:NE:2]))
                do(dve.tensor_scalar(row_g[:, 0:PAIRS], row_f[:, 0:PAIRS], 0.0, float(4 * S), ALU.is_equal, ALU.mult))
                do(dve.scalar_tensor_tensor(row_f[:, 0:PAIRS], row_f[:, 0:PAIRS], -1.0, row_g[:, 0:PAIRS], ALU.add, ALU.add))
                dve.tensor_copy(row_i[:], row_f[:, 0:PAIRS]).then_inc(tok_ready.sem, 1)

                def gained(k, q, half):
                    dve.wait_ge(g_flip.sem, g_flip.at(L, k + 1))
                    for g in range(2):
                        c = 4 * half + 2 * g
                        gain = g_norm[:, 1, L, c:c + 2].unsqueeze(2).to_broadcast([P, 2, 2 * P])
                        dve.tensor_tensor(xgT[q][:, c:c + 2], ps(g).rearrange("p (a b) -> p a b", a=2), gain,
                                          ALU.mult).then_inc(xgT_ready.sem, 1)

                def pair(n, r, more, further):
                    b = r % 2
                    dve.wait_ge(silu_done.sem, silu_done.at(L, n + 1))
                    dve.tensor_tensor(hid[b].rearrange("p (j q) -> p q j", j=EC),
                                      silu[b].rearrange("p (q j) -> p q j", j=EC),
                                      ps(2 + b, DE, off=DE).rearrange("p (q j) -> p q j", j=EC), ALU.mult).then_inc(hid_ready.sem, 1)
                    if more:
                        gained(n + 2, (r // 2 + 1) % 2, b)
                    if further:
                        select(n + 3, 0)
                        select(n + 4, 1)
                    dve.wait_ge(dn_done.sem, dn_done.at(L, n + 1))
                    dve.wait_ge(y_free.sem, y_free.at(L, n))
                    dve.tensor_copy(y_out[b][:, 0:HALF], ps(6)).then_inc(y_dve.sem, 1)

                gained(0, 0, 0)
                gained(1, 0, 1)
                select(2, 0)
                select(3, 1)
                do(dve.tensor_tensor(steps7, ps(5, NE, off=NT * NE).unsqueeze(2).to_broadcast([P, NE, 7]),
                                     thresh[:].unsqueeze(1).to_broadcast([P, NE, 7]), ALU.is_gt))
                do(dve.tensor_reduce(extra, steps7, axis=AX.X, op=ALU.add))
                do(dve.tensor_tensor_scan(extra_sum, extra, ones[:, 0:1].to_broadcast([P, NE]), 0.0, ALU.add, ALU.mult))
                do(dve.tensor_tensor(xtra_f[:, 0:1], xtra_f[:, 0:1], xtra_f[:, 1:2], ALU.add))
                do(dve.tensor_copy(xtra_f[:, 1:2], extra_sum[:, NE - 1:NE]))
                do(dve.tensor_tensor(steps15, extra_sum.unsqueeze(1).to_broadcast([P, 16, NE]),
                                     xtra_no[:].unsqueeze(2).to_broadcast([P, 16, NE]), ALU.is_le))
                do(dve.tensor_reduce(xtra_f[:, 2:18], steps15, axis=AX.X, op=ALU.add))
                do(dve.tensor_scalar(xtra_f[:, 2:18], xtra_f[:, 2:18], float(NE - 1), None, ALU.min))
                do(dve.tensor_copy(xtra_i[:], xtra_f[:]))
                do(dve.tensor_tensor(shift, extra_sum, extra, ALU.subtract))
                do(dve.tensor_tensor(shift, shift, expert_no[:], ALU.subtract))
                do(dve.tensor_scalar(shift, shift, float(SLOT), float(MAIN - SLOT), ALU.mult, ALU.add))
                do(dve.tensor_scalar(over, rank, float(SLOT), None, ALU.is_ge))
                do(dve.tensor_tensor(over, over, shift.unsqueeze(1).to_broadcast(four), ALU.mult))
                do(dve.tensor_tensor(rtmp, rank, over, ALU.add))
                do(dve.scalar_tensor_tensor(rtmp, e_bc, float(SLOT), rtmp, ALU.mult, ALU.add))
                for a in range(2):
                    do(dve.tensor_tensor(over, chosen[:, a], rtmp, ALU.mult))
                    do(dve.tensor_reduce(slot_f[:, a], over, axis=AX.X, op=ALU.add))
                dve.tensor_scalar(slot_f[:], slot_f[:], float(-MAIN), None, ALU.add).then_inc(slots_ready.sem, 1)
                dve.wait_ge(slots_ready.sem, slots_ready.at(L, 1))
                alone(dve)

                with dve.Fori(0, PAIRS // 4 - 1) as i:
                    for r in range(4):
                        pair(4 * i + r, r, True, r % 2 == 1)
                for r in range(4):
                    pair(PAIRS - 4 + r, r, r < 2, False)
                dve.wait_ge(y_free.sem, y_free.at(L, PAIRS + 1))
                alone(dve)
                so_far = dve.value_load(xtra_i[0:1, 0:1], min_val=0, max_val=DEPTH * XTRA)
                n_xtra = dve.value_load(xtra_i[0:1, 1:2], min_val=0, max_val=XTRA)
                with dve.If(n_xtra > 0):
                    with dve.Fori(0, XTRA) as j:
                        with dve.If(j < n_xtra):
                            dve.tensor_tensor(sel_x, pair_slot[:, 0:SLOT].unsqueeze(1).to_broadcast([P, 2 * NT, SLOT]),
                                              slot_f[:].rearrange("p a t -> p (a t)").unsqueeze(2).to_broadcast([P, 2 * NT, SLOT]),
                                              ALU.is_equal).then_inc(x_sel, 1)
                            dve.tensor_tensor(sel_half, by_slot, slots_of(slot_f, 0), ALU.is_equal).then_inc(x_sel, 1)
                            dve.tensor_tensor(sel_other, by_slot, slots_of(slot_f, 1), ALU.is_equal).then_inc(x_sel, 1)
                            dve.wait_ge(x_sel, 5 * (so_far + j) + 3)
                            dve.tensor_scalar(slot_f[:], slot_f[:], float(-SLOT), None, ALU.add).then_inc(x_sel, 1)
                            dve.tensor_tensor(sel[:, :, 0:P], sel_other, sel_half, ALU.add).then_inc(x_sel, 1)
                            dve.wait_ge(x_sel, 5 * (so_far + j) + 5)
                            dve.wait_ge(x_tok, so_far + j + 1)
                            dve.tensor_copy(row_f[0:SLOT, PAIRS:], ps(4, 1, hi=SLOT)).then_inc(x_row, 1)
                            dve.wait_ge(x_row, 3 * (so_far + j) + 1)
                            dve.tensor_scalar(row_g[0:SLOT, PAIRS:], row_f[0:SLOT, PAIRS:], 0.0, float(4 * S), ALU.is_equal, ALU.mult).then_inc(x_row, 1)
                            dve.wait_ge(x_row, 3 * (so_far + j) + 2)
                            dve.scalar_tensor_tensor(row_f[0:SLOT, PAIRS:], row_f[0:SLOT, PAIRS:], -1.0, row_g[0:SLOT, PAIRS:], ALU.add, ALU.add).then_inc(x_row, 1)
                            dve.wait_ge(x_row, 3 * (so_far + j) + 3)
                            dve.tensor_copy(rowx_i[0:SLOT, :], row_f[0:SLOT, PAIRS:]).then_inc(x_idx, 1)
                            dve.wait_ge(x_flip, so_far + j + 1)
                            for g in range(2):
                                dve.tensor_tensor(xgT[0][:, 4 * g:4 * g + 4, 0:P], ps(g).rearrange("p (a b) -> p a b", a=4),
                                                  g_norm[:, 1, L, 4 * g:4 * g + 4].unsqueeze(2).to_broadcast([P, 4, P]), ALU.mult).then_inc(x_T, 1)
                            dve.wait_ge(x_silu, so_far + j + 1)
                            dve.tensor_tensor(hid[0][0:SLOT].rearrange("p (j q) -> p q j", j=EC),
                                              silu[0][0:SLOT].rearrange("p (q j) -> p q j", j=EC),
                                              ps(2, DE, off=DE, hi=SLOT).rearrange("p (q j) -> p q j", j=EC), ALU.mult).then_inc(x_hid, 1)
                            dve.wait_ge(x_hflip, so_far + j + 1)
                            dve.tensor_copy(hidT[0][:, :, 0:SLOT], ps(5, EC * SLOT).rearrange("p (a b) -> p a b", a=EC)).then_inc(x_hT, 1)
                            dve.wait_ge(x_dn, so_far + j + 1)
                            dve.tensor_copy(y_out[0][0:SLOT], ps2(6, D)[0:SLOT]).then_inc(x_y, 1)
                            dve.wait_ge(x_store, 16 * (so_far + j + 1))
                            alone(dve)
                        dve.nop()
                dve.nop()
                def combine(t):
                    dve.wait_ge(back_in[t].sem, back_in[t].at(L, 16))
                    dve.scalar_tensor_tensor(h[:, t], back[t % 3][:, 0], top_w[:, 0, t:t + 1], h[:, t], ALU.mult,
                                             ALU.add).then_inc(step.add(L), 1)
                    step.wait(L)
                    dve.scalar_tensor_tensor(h[:, t], back[t % 3][:, 1], top_w[:, 1, t:t + 1], h[:, t], ALU.mult,
                                             ALU.add).then_inc(h_moe.sem, 1)

                def embed(k):
                    part = h[:, k // 2, (k % 2) * HALF:(k % 2 + 1) * HALF]
                    dve.wait_ge(gate_out.sem, gate_out.at(L, k + 1))
                    dve.wait_ge(emb_out.sem, emb_out.at(L, k + 1))
                    dve.tensor_tensor(gate_s[k % 2], gate_s[k % 2], emb[:, k // 2, (k % 2) * HALF:(k % 2 + 1) * HALF], ALU.mult).then_inc(step.add(L), 1)
                    step.wait(L)
                    dve.tensor_tensor(part, part, gate_s[k % 2], ALU.add).then_inc(ple_out.sem, 1)

                combine(0)
                scaled(2, 0)
                combine(1)
                turned(2, 0, 0)
                scaled(2, 1)
                combine(2)
                scaled(2, 2)
                combine(3)
                turned(2, 1, 2)
                scaled(2, 3)
                embed(0)
                embed(1)
                turned(2, 2, 0)
                embed(2)
                embed(3)
                turned(2, 3, 2)
                for k in range(4, 2 * NT):
                    embed(k)
            assert step.n == STEPS_DVE, step.n
            dve.wait_ge(g_last_in.sem, 16)
            for t in range(NT):
                dve.wait_ge(fin_root.sem, t + 1)
                dve.scalar_tensor_tensor(h[:, t], h[:, t], rstd[:, 12 + t:13 + t], g_last, ALU.mult, ALU.mult).then_inc(fin_ready.sem, 1)

        @block.tensor
        def _(pe):
            pe.wait_ge(const_ready.sem, 1)

            with pe.Fori(0, DEPTH) as L:

                def turn_tile(stage, t, b):
                    pe.wait_ge(xn_ready.sem, xn_ready.at(L, stage * NT + t + 1))
                    for c in range(DC):
                        last = pe.transpose(ps(b + c // 4, P, off=(c % 4) * P), xn[t % 2][:, c * P:(c + 1) * P], ident[:])
                    last.then_inc(flipped.sem, 1)

                def norm(stage):
                    for t in range(NT):
                        if t >= 2:
                            pe.wait_ge(xT_ready.sem, xT_ready.at(L, 2 * (stage * NT + t - 1)))
                        turn_tile(stage, t, 2 * (t % 2))

                norm(0)
                pe.wait_ge(x_lo_ready.sem, x_lo_ready.at(L, NT))
                pe.wait_ge(ple_out.sem, ple_out.at(L, 0))
                for k in range(QK_UNITS):
                    m, ch = k // 2, k % 2
                    if m >= 4 and ch == 0:
                        freed = (qk_act, qk_dve)[m % 2]
                        pe.wait_ge(freed.sem, freed.at(L, (m - 4) // 2 + 1))
                    pe.wait_ge(lo_ready.sem, lo_ready.at(L, k + 1))
                    hi, lo = unit_part(w_hi, k), unit_part(w_lo, k)
                    for c in range(4):
                        for j, (w, x) in enumerate(((hi, x_hi), (hi, x_lo), (lo, x_hi))):
                            last = pe.matmul(ps(4 + m % 4), w[:, c], x[:, 4 * ch + c], start=(ch == 0 and c == 0 and j == 0),
                                             stop=(ch == 1 and c == 3 and j == 2))
                    last.then_inc(in_done.sem, 1)
                for k in range(QK_UNITS, IN_UNITS):
                    g, c = (k - QK_UNITS) // DC, (k - QK_UNITS) % DC
                    if g == 1 and c == 0:
                        pe.wait_ge(qk_act.sem, qk_act.at(L, NPAIR))
                        pe.wait_ge(qk_dve.sem, qk_dve.at(L, NPAIR))
                    if g == 2 and c == 0:
                        pe.wait_ge(lat_out.sem, lat_out.at(L, NT))
                    pe.wait_ge(lo_ready.sem, lo_ready.at(L, k + 1))
                    hi, lo = unit_part(w_hi, k), unit_part(w_lo, k)
                    for t in range(NT):
                        for j, (x, w) in enumerate(((x_hi, hi), (x_lo, hi), (x_hi, lo))):
                            last = pe.matmul(ps(4 * (g % 2) + t, GROUPS[g][1]), x[:, c, t * P:(t + 1) * P], w,
                                             start=(c == 0 and j == 0), stop=(c == DC - 1 and j == 2))
                    last.then_inc(in_done.sem, 1)
                pe.wait_ge(v_out.sem, v_out.at(L, NT))
                pe.wait_ge(lat_out.sem, lat_out.at(L, 2 * NT))
                for t in range(NT):
                    pe.wait_ge(lat_ready.sem, lat_ready.at(L, t + 1))
                    for j in range(QC + KVC):
                        last = pe.transpose(ps(3 + j, P, off=t * P), lat[:, t, j * P:(j + 1) * P], ident[:])
                last.then_inc(lat_flip.sem, 1)

                def scores(u, q, k, depth, scale_mask, done):
                    m, qb = u // NT, u % NT
                    n = (qb + 1) * P
                    for s in range(2):
                        z = ps(2 * (u % 2) + s, n)
                        pe.matmul(z, q(m, s, qb), k(m, s, n), start=True, stop=False)
                        last = pe.matmul(ps(2 * (u % 2) + s, P, off=n - P), ident_b[:], scale_mask[:], start=False, stop=True)
                    last.then_inc(done.sem, 1)

                def flip(u, w, done):
                    for s in range(2):
                        for kb in range(keys(u) // P):
                            last = pe.transpose(ps(4 + s, P, off=kb * P), w(u, s, kb), ident[:])
                    last.then_inc(done.sem, 1)

                def outputs(u, w, done):
                    m, qb = u // NT, u % NT
                    for kb in range(qb + 1):
                        for s in range(2):
                            hd = 2 * m + s
                            last = pe.matmul(ps(6 + m % 2, P, off=qb * P, lo=HD * s, hi=HD * (s + 1)),
                                             v_att[:, kb, hd * HD:(hd + 1) * HD], w[:, u % 2, s, kb * P:(kb + 1) * P],
                                             start=(kb == 0), stop=(kb == qb), skip_group_check=True)
                    last.then_inc(done.sem, 1)

                def attention(q, k, depth, mask, kind, z_done, z_used, w_ready, flipped_, wT_ready, wT_, weights, o_done):
                    for u in range(2):
                        scores(u, q, k, depth, mask, z_done)
                    for u in range(UNITS):
                        pe.wait_ge(w_ready.sem, w_ready.at(L, 2 * u + 2))
                        if u:
                            for s in range(2):
                                pe.wait_ge(wT_ready[s].sem, wT_ready[s].at(L, u))
                        flip(u, weights, flipped_)
                        if u + 2 < UNITS:
                            pe.wait_ge(z_used.sem, z_used.at(L, 2 * u + 2))
                            scores(u + 2, q, k, depth, mask, z_done)
                        for s in range(2):
                            pe.wait_ge(wT_ready[s].sem, wT_ready[s].at(L, u + 1))
                        m = u // NT
                        if u % NT == 0 and m >= 2:
                            pe.wait_ge(o_sq.sem, o_sq.at(L, kind * NPAIR + m - 1))
                        outputs(u, wT_, o_done)

                pe.wait_ge(cqT_ready.sem, cqT_ready.at(L, 1))
                pe.wait_ge(ckvT_ready.sem, ckvT_ready.at(L, 1))
                attention(lambda m, s, qb: qT_sb[HD * s:HD * (s + 1), m, qb * P:(qb + 1) * P],
                          lambda m, s, n: kT_sb[HD * s:HD * (s + 1), m, 0:n], HD, sb_mask, 0, sb_z, sb_sig, sb_w, sb_flip,
                          sb_wT, wT, lambda u, s, kb: take[:, u % 2, s, S - keys(u) + kb * P:S - keys(u) + (kb + 1) * P],
                          sb_o)
                pe.wait_ge(w_up_in.sem, w_up_in.at(L, 2 * 16))
                pe.wait_ge(sb_sig.sem, sb_sig.at(L, 2 * UNITS))
                for t in range(NT + 1):
                    if t < NT:
                        if t:
                            pe.wait_ge(q_out.sem, q_out.at(L, t))
                        for lo, n in ((0, 512), (512, NH * QK - 512)):
                            for j in range(QC):
                                last = pe.matmul(ps(lo // 512, n), cqT[:, j, t * P:(t + 1) * P], w_uq[:, j, lo:lo + n],
                                                 start=(j == 0), stop=(j == QC - 1))
                        last.then_inc(up_done.sem, 1)
                        if t:
                            pe.wait_ge(k_out.sem, k_out.at(L, t))
                        for lo in (0, 512):
                            for j in range(KVC):
                                last = pe.matmul(ps(2 + lo // 512), ckvT[:, j, t * P:(t + 1) * P], w_ukv[:, j, lo:lo + 512],
                                                 start=(j == 0), stop=(j == KVC - 1))
                        last.then_inc(up_done.sem, 1)
                    if t == 0:
                        pe.wait_ge(o_sum.sem, o_sum.at(L, NPAIR))
                        for k in range(NT):
                            last = pe.matmul(ps(7, 1, off=k), o_total[0][:, k * P:(k + 1) * P], ones[:, 0:1], start=True, stop=True)
                        last.then_inc(o_ms.sem, 1)
                    else:
                        v = t - 1
                        pe.wait_ge(q_rope.sem, q_rope.at(L, v + 1))
                        if v:
                            pe.wait_ge(qT_out.sem, qT_out.at(L, 2 * v))
                        for hd in range(NH):
                            last = pe.transpose(ps(4 + hd // 4, P, off=(hd % 4) * P, hi=QK), q_tok[:, hd], ident[:])
                        last.then_inc(up_flip.sem, 1)
                        pe.wait_ge(k_rope.sem, k_rope.at(L, v + 1))
                        if v:
                            pe.wait_ge(kT_out.sem, kT_out.at(L, 2 * v))
                        else:
                            pe.wait_ge(o_ms_out.sem, o_ms_out.at(L, 1))
                        for hd in range(NH):
                            last = pe.transpose(ps(6 + hd // 4, P, off=(hd % 4) * P, hi=QK), k_tok[:, hd], ident[:])
                        last.then_inc(up_flip.sem, 1)
                pe.wait_ge(qT_out.sem, qT_out.at(L, 2 * NT))
                pe.wait_ge(kT_out.sem, kT_out.at(L, 2 * NT))
                attention(lambda m, s, qb: qT[0:QK, 2 * m + s, qb * P:(qb + 1) * P],
                          lambda m, s, n: kT[0:QK, 2 * m + s, 0:n], QK, mla_mask, 1, ml_z, ml_exp, ml_w, ml_flip,
                          ml_wT, pTr, lambda u, s, kb: prob[:, u % 2, s, kb * P:(kb + 1) * P], ml_o)
                pe.wait_ge(w_o_in.sem, w_o_in.at(L, 16))
                pe.wait_ge(o_sq.sem, o_sq.at(L, NPAIR))
                def route(t):
                    pe.wait_ge(xT_ready.sem, xT_ready.at(L, 2 * NT + 2 * (t + 1)))
                    for c in range(DC):
                        last = pe.matmul(ps(4, NR, off=t * NR), xT[:, c, t * P:(t + 1) * P], w_r[:, c], start=(c == 0), stop=(c == DC - 1))
                    last.then_inc(r_done.sem, 1)

                pe.wait_ge(r_in.sem, r_in.at(L, 2 * 16))
                for k in range(2 * NT):
                    t, half = k // 2, k % 2
                    if k >= 2:
                        pe.wait_ge(wo_out.sem, wo_out.at(L, k - 1))
                    for kind in range(2):
                        if k == 0 and kind == 1:
                            pe.wait_ge(o_sq.sem, o_sq.at(L, 2 * NPAIR))
                        for m in range(NPAIR):
                            c = kind * NPAIR + m
                            last = pe.matmul(ps(2 * (k % 2) + kind), oT[:, c, t * P:(t + 1) * P],
                                             w_o[:, c, half * HALF:(half + 1) * HALF], start=(m == 0), stop=(m == NPAIR - 1))
                    last.then_inc(wo_done.sem, 1)
                    if k == 0:
                        pe.wait_ge(o_sum.sem, o_sum.at(L, 2 * NPAIR))
                        for v in range(NT):
                            last = pe.matmul(ps(5, 1, off=v), o_total[1][:, v * P:(v + 1) * P], ones[:, 0:1], start=True, stop=True)
                        last.then_inc(o_ms.sem, 1)
                    if half == 0 and t:
                        if t >= 2:
                            pe.wait_ge(xT_ready.sem, xT_ready.at(L, 2 * (NT + t - 1)))
                        turn_tile(1, t - 1, 6)
                    if half == 1 and t:
                        route(t - 1)
                pe.wait_ge(xT_ready.sem, xT_ready.at(L, 2 * (2 * NT - 1)))
                turn_tile(1, NT - 1, 6)
                route(NT - 1)
                pe.wait_ge(memb_ready.sem, memb_ready.at(L, 1))
                for t in range(NT + 1):
                    n = min(t, NT - 1)
                    for k in range(n + 1):
                        last = pe.matmul(ps(5, NE, off=t * NE), before_b[:] if k == t else ones_b[:], memb_b[:, k],
                                         start=(k == 0), stop=(k == n))
                last.then_inc(rank_done.sem, 1)
                def tokens(k, q, half, first=False):
                    pe.wait_ge(selected.sem, selected.at(L, k - half + 2))
                    if not first:
                        pe.wait_ge(xgT_ready.sem, xgT_ready.at(L, 2 * k))
                    for c in range(4 * half, 4 * half + 4):
                        for v in range(2 * NT):
                            last = pe.matmul(ps(c // 2 % 2, 2 * P, off=(c % 2) * 2 * P), x_parts[:, v // NT, v % NT, c * P:(c + 1) * P],
                                             sel[:, v % NT], start=(v == 0), stop=(v == 2 * NT - 1))
                    last.then_inc(g_flip.sem, 1)

                def pair(n, i, r, more):
                    q, b = r // 2, r % 2
                    pe.wait_ge(xgT_ready.sem, xgT_ready.at(L, 2 * (n - b + 2)))
                    pe.wait_ge(gu_in[b].sem, gu_in[b].at(L, 32 * (i + 1)))
                    for c in range(DC):
                        for e in range(2):
                            last = pe.matmul(ps(2 + b, lo=SLOT * e, hi=SLOT * (e + 1)), xgT[q][:, c, P * b + SLOT * e:P * b + SLOT * (e + 1)],
                                             w_gu[2 * b + e][:, :, c], start=(c == 0), stop=(c == DC - 1), skip_group_check=True)
                    last.then_inc(gu_done.sem, 1)
                    if more:
                        tokens(n + 2, 1 - q, b)
                    pe.wait_ge(hid_ready.sem, hid_ready.at(L, n + 1))
                    for j in range(EC):
                        last = pe.transpose(ps(5, P, off=j * P), hid[b][:, j * P:(j + 1) * P], ident[:])
                    last.then_inc(hid_flip.sem, 1)
                    pe.wait_ge(hidT_ready.sem, hidT_ready.at(L, n + 1))
                    pe.wait_ge(dn_in[b].sem, dn_in[b].at(L, 16 * (i + 1)))
                    pe.wait_ge(y_act.sem, y_act.at(L, n))
                    pe.wait_ge(y_dve.sem, y_dve.at(L, n))
                    for half in range(2):
                        for j in range(EC):
                            for e in range(2):
                                last = pe.matmul(ps(6 + half, lo=SLOT * e, hi=SLOT * (e + 1)), hidT[b][:, j, SLOT * e:SLOT * (e + 1)],
                                                 w_dn[2 * b + e][:, j, half * HALF:(half + 1) * HALF],
                                                 start=(j == 0), stop=(j == EC - 1), skip_group_check=True)
                    last.then_inc(dn_done.sem, 1)

                pe.wait_ge(part_lo.sem, part_lo.at(L, NT))
                tokens(0, 0, 0, first=True)
                pe.wait_ge(sel_ready.sem, sel_ready.at(L, 1))
                for k in range(2 * NT):
                    last = pe.matmul(ps(6, NE), sel_rank[:, k], sel_tok[:, k], start=(k == 0), stop=(k == 2 * NT - 1))
                last.then_inc(tok_done.sem, 1)
                tokens(1, 0, 1)
                with pe.Fori(0, PAIRS // 4 - 1) as i:
                    for r in range(4):
                        pair(4 * i + r, 2 * i + r // 2, r, True)
                for r in range(4):
                    pair(PAIRS - 4 + r, PAIRS // 2 - 2 + r // 2, r, r < 2)
                pe.wait_ge(y_act.sem, y_act.at(L, PAIRS))
                pe.wait_ge(y_dve.sem, y_dve.at(L, PAIRS))
                pe.wait_ge(w_e_in.sem, w_e_in.at(L, 2 * 16))
                for j in range(PC):
                    for t in range(NT):
                        last = pe.transpose(ps(4 + j, P, off=t * P), p_tok[:, t, j:PE_IN:PC], ident[:])
                    last.then_inc(p_flip.sem, 1)
                pe.wait_ge(pT_ready.sem, pT_ready.at(L, PC))
                pe.wait_ge(slots_ready.sem, slots_ready.at(L, 1))
                alone(pe)
                so_far = pe.value_load(xtra_i[0:1, 0:1], min_val=0, max_val=DEPTH * XTRA)
                n_xtra = pe.value_load(xtra_i[0:1, 1:2], min_val=0, max_val=XTRA)
                with pe.If(n_xtra > 0):
                    with pe.Fori(0, XTRA) as j:
                        with pe.If(j < n_xtra):
                            pe.wait_ge(x_sel, 5 * (so_far + j) + 5)
                            for k in range(2 * NT):
                                last = pe.matmul(ps(4, 1, hi=SLOT), sel_x[:, k], row_no[:, k // NT, k % NT:k % NT + 1], start=(k == 0), stop=(k == 2 * NT - 1))
                            last.then_inc(x_tok, 1)
                            for c in range(DC):
                                for k in range(2 * NT):
                                    last = pe.matmul(ps(c // 4, P, off=(c % 4) * P), x_parts[:, k // NT, k % NT, c * P:(c + 1) * P],
                                                     sel[:, k % NT, 0:P], start=(k == 0), stop=(k == 2 * NT - 1))
                            last.then_inc(x_flip, 1)
                            pe.wait_ge(x_T, 2 * (so_far + j) + 2)
                            pe.wait_ge(x_w, 48 * (so_far + j + 1))
                            for c in range(DC):
                                last = pe.matmul(ps(2, hi=SLOT), xgT[0][:, c, 0:SLOT], w_gu[2][:, :, c], start=(c == 0), stop=(c == DC - 1))
                            last.then_inc(x_gu, 1)
                            pe.wait_ge(x_hid, so_far + j + 1)
                            alone(pe)
                            for k in range(EC):
                                last = pe.transpose(ps(5, SLOT, off=k * SLOT), hid[0][0:SLOT, k * P:(k + 1) * P], ident[0:SLOT, 0:SLOT])
                            last.then_inc(x_hflip, 1)
                            pe.wait_ge(x_hT, so_far + j + 1)
                            for half in range(2):
                                for k in range(EC):
                                    last = pe.matmul(ps(6 + half, hi=SLOT), hidT[0][:, k, 0:SLOT], w_dn[2][:, k, half * HALF:(half + 1) * HALF],
                                                     start=(k == 0), stop=(k == EC - 1))
                            last.then_inc(x_dn, 1)
                        pe.nop()
                pe.nop()
                for k in range(2 * NT):
                    t, cols = k // 2, slice((k % 2) * HALF, (k % 2 + 1) * HALF)
                    if k >= 2:
                        pe.wait_ge(emb_out.sem, emb_out.at(L, k - 1))
                    for j in range(PC):
                        last = pe.matmul(ps(4 + k % 2), pT[:, j, t * P:(t + 1) * P], w_e[:, j, cols], start=(j == 0), stop=(j == PC - 1))
                    last.then_inc(emb_done.sem, 1)
                turn_tile(2, 0, 0)
                pe.wait_ge(w_g_last_in.sem, w_g_last_in.at(L, 16))
                for k in range(2 * NT):
                    t, cols = k // 2, slice((k % 2) * HALF, (k % 2 + 1) * HALF)
                    if k % 2 == 0:
                        pe.wait_ge(xT_ready.sem, xT_ready.at(L, 4 * NT + 2 * (t + 1)))
                    if k >= 2:
                        pe.wait_ge(gate_out.sem, gate_out.at(L, k - 1))
                    if k < 2:
                        pe.wait_ge(w_g_in[k].sem, w_g_in[k].at(L, 16))
                    for c in range(DC):
                        weights = w_g[:, c, cols] if c < DC - 1 else w_g_last[:, cols]
                        last = pe.matmul(ps(6 + k % 2), xT[:, c, t * P:(t + 1) * P], weights, start=(c == 0), stop=(c == DC - 1))
                    last.then_inc(gate_done.sem, 1)
                    if k % 2 == 0 and t < NT - 1:
                        if t:
                            pe.wait_ge(xT_ready.sem, xT_ready.at(L, 2 * (2 * NT + t)))
                        turn_tile(2, t + 1, 2 * ((t + 1) % 2))


_INS = ["x", "p", "positions", "g_mix", "w_in", "g_cq", "w_uq", "g_ckv", "w_ukv", "g_osb", "g_omla", "w_out", "g_moe",
        "w_rg", "b_rg", "w_re", "b_re", "w_gate", "w_up", "w_down", "g_ple", "w_pg", "w_pe", "g_final"]


def kernel(**inputs):
    import numpy as np
    import concourse.bacc as bacc
    from concourse import mybir
    from concourse.bass_utils import run_bass_kernel_spmd

    nc = bacc.Bacc("TRN2", target_bir_lowering=False, num_devices=1)
    arrays, io = {}, {}
    for name in _INS:
        a = np.ascontiguousarray(inputs[name])
        arrays[f"in_{name}"] = a
        io[name] = nc.dram_tensor(f"in_{name}", a.shape, mybir.dt.from_np(a.dtype), kind="ExternalInput").ap()
    shape = inputs["x"].shape
    out = nc.dram_tensor("out_trunk", shape, mybir.dt.float32, kind="ExternalOutput").ap()
    _program(nc, io, out)
    r = run_bass_kernel_spmd(nc, [arrays], core_ids=[0])
    return r.results[0]["out_trunk"]
```
